# Optimizing a Trainium2 kernel written in Bass

```python
import math, functools
import jax, jax.numpy as jnp
from jax import lax
import numpy as np

D_MODEL = 1024
BATCH = 1
SEQ = 1024
DEPTH = 2
DEC_BATCH = 8
DEC_SEQ = 4
PAST_LEN = 1024
PAGE_SIZE = 128

MIX_WIDTH = D_MODEL
GLA_WIDTH = D_MODEL // 2
GLA_HEADS = 4
GLA_DV = GLA_WIDTH // GLA_HEADS
GLA_DK = GLA_DV // 2
GLA_QK = GLA_HEADS * GLA_DK
GATE_RANK = 16
GATE_NORMALIZER = 16.0
GLA_CHUNK = 64
SWA_HEAD_DIM = 64
SWA_HEADS = (MIX_WIDTH - GLA_WIDTH) // SWA_HEAD_DIM
SWA_KV_HEADS = SWA_HEADS // 4
SWA_GROUP = SWA_HEADS // SWA_KV_HEADS
WINDOW = 128
ROPE_THETA = 10000.0
D_FF = ((8 * D_MODEL // 3 + 255) // 256) * 256
NORM_EPS = 1e-6

_IN_SIZES = (GLA_QK, GLA_QK, GLA_WIDTH, GATE_RANK, GLA_WIDTH,
             SWA_HEADS * SWA_HEAD_DIM, SWA_KV_HEADS * SWA_HEAD_DIM, SWA_KV_HEADS * SWA_HEAD_DIM)
IN_COLS = sum(_IN_SIZES)
_SPLITS = tuple(int(s) for s in np.cumsum(_IN_SIZES)[:-1])

kernel_name = "hymba_gla_swa_sink_decoder_step"

def _rmsnorm(x, g):
    xf = x.astype(jnp.float32)
    y = xf * lax.rsqrt(jnp.mean(xf * xf, axis=-1, keepdims=True) + NORM_EPS)
    return (y * g.astype(jnp.float32)).astype(x.dtype)

def _rope(x, pos):
    half = x.shape[-1] // 2
    inv = ROPE_THETA ** (-jnp.arange(half, dtype=jnp.float32) / half)
    ang = pos.astype(jnp.float32)[:, None] * inv[None, :]
    cos = jnp.cos(ang)[None, :, None, :]
    sin = jnp.sin(ang)[None, :, None, :]
    xf = x.astype(jnp.float32)
    x1, x2 = xf[..., :half], xf[..., half:]
    return jnp.concatenate([x1 * cos - x2 * sin, x2 * cos + x1 * sin], axis=-1).astype(x.dtype)

def _gla(q, k, v, g, S0):
    B, T, H, K = q.shape
    V = v.shape[-1]
    C = math.gcd(T, GLA_CHUNK)
    n = T // C
    causal = jnp.tril(jnp.ones((C, C), dtype=bool))[None, :, :, None, None]

    def to_chunks(a):
        return a.reshape(B, n, C, H, a.shape[-1]).swapaxes(0, 1)

    def step(S, inp):
        qc, kc, vc, gc = inp
        b = jnp.cumsum(gc, axis=1)
        o_inter = jnp.einsum('bthk,bhkv->bthv', qc * jnp.exp(b), S)
        diff = b[:, :, None] - b[:, None, :]
        decay = jnp.where(causal, jnp.exp(jnp.where(causal, diff, 0.0)), 0.0)
        A = jnp.einsum('bthk,btshk,bshk->bhts', qc, decay, kc)
        o_intra = jnp.einsum('bhts,bshv->bthv', A, vc)
        b_last = b[:, -1]
        k_dec = kc * jnp.exp(b_last[:, None] - b)
        S_new = jnp.exp(b_last)[..., None] * S + jnp.einsum('bshk,bshv->bhkv', k_dec, vc)
        return S_new, o_inter + o_intra

    S, o = lax.scan(step, S0, (to_chunks(q), to_chunks(k), to_chunks(v), to_chunks(g)))
    return o.swapaxes(0, 1).reshape(B, T, H, V), S

def _sink_attention(q, k, v, sinks, qpos, kpos):
    hd = q.shape[-1]
    s = jnp.einsum('bnqkgd,bnskd->bnkgqs', q.astype(jnp.float32), k.astype(jnp.float32)) * (hd ** -0.5)
    diff = qpos[:, :, None] - kpos[:, None, :]
    mask = (diff >= 0) & (diff < WINDOW) & (kpos[:, None, :] >= 0)
    s = jnp.where(mask[None, :, None, None], s, -jnp.inf)
    sink = sinks.astype(jnp.float32).reshape(1, 1, SWA_KV_HEADS, SWA_GROUP, 1, 1)
    m = jnp.maximum(jnp.max(s, axis=-1, keepdims=True), sink)
    p = jnp.exp(s - m)
    denom = jnp.sum(p, axis=-1, keepdims=True) + jnp.exp(sink - m)
    return jnp.einsum('bnkgqs,bnskd->bnqkgd', p / denom, v.astype(jnp.float32))

def _swa_prompt(q, k, v, sinks):
    B, T = q.shape[0], q.shape[1]
    N = T // WINDOW
    qb = q.reshape(B, N, WINDOW, SWA_KV_HEADS, SWA_GROUP, SWA_HEAD_DIM)
    kb = k.reshape(B, N, WINDOW, SWA_KV_HEADS, SWA_HEAD_DIM)
    vb = v.reshape(B, N, WINDOW, SWA_KV_HEADS, SWA_HEAD_DIM)
    kk = jnp.concatenate([jnp.concatenate([jnp.zeros_like(kb[:, :1]), kb[:, :-1]], axis=1), kb], axis=2)
    vv = jnp.concatenate([jnp.concatenate([jnp.zeros_like(vb[:, :1]), vb[:, :-1]], axis=1), vb], axis=2)
    qpos = jnp.arange(T).reshape(N, WINDOW)
    kpos = (jnp.arange(N)[:, None] - 1) * WINDOW + jnp.arange(2 * WINDOW)[None, :]
    o = _sink_attention(qb, kk, vv, sinks, qpos, kpos)
    w_buf = min(WINDOW, PAST_LEN)
    return o.reshape(B, T, SWA_HEADS * SWA_HEAD_DIM), k[:, -w_buf:], v[:, -w_buf:]

def _swa_sample(q, k, v, sinks, kbuf, vbuf):
    B, T = q.shape[0], q.shape[1]
    W = kbuf.shape[1]
    keys = jnp.concatenate([kbuf.astype(k.dtype), k], axis=1)
    vals = jnp.concatenate([vbuf.astype(v.dtype), v], axis=1)
    qpos = (PAST_LEN + jnp.arange(T))[None]
    kpos = (PAST_LEN - W + jnp.arange(W + T))[None]
    o = _sink_attention(q.reshape(B, 1, T, SWA_KV_HEADS, SWA_GROUP, SWA_HEAD_DIM),
                        keys[:, None], vals[:, None], sinks, qpos, kpos)
    return o.reshape(B, T, SWA_HEADS * SWA_HEAD_DIM), keys[:, -W:], vals[:, -W:]

def _layer(x, pos, S0, attend, norm_attn, w_in, w_gk2, b_gk2, gla_norm, sinks, w_o,
           norm_ffn, w_gate, w_up, w_down):
    B, T, _ = x.shape
    f32 = jnp.float32
    h = _rmsnorm(x, norm_attn)
    z = h @ w_in
    gq, gk, gv, ga, gg, sq, sk, sv = jnp.split(z, _SPLITS, axis=-1)
    q = gq.reshape(B, T, GLA_HEADS, GLA_DK).astype(f32) * (GLA_DK ** -0.5)
    k = gk.reshape(B, T, GLA_HEADS, GLA_DK).astype(f32)
    v = gv.reshape(B, T, GLA_HEADS, GLA_DV).astype(f32)
    g = jax.nn.log_sigmoid((ga @ w_gk2 + b_gk2).astype(f32)) / GATE_NORMALIZER
    o, S = _gla(q, k, v, g.reshape(B, T, GLA_HEADS, GLA_DK), S0.astype(f32))
    o = _rmsnorm(o, gla_norm) * jax.nn.silu(gg.reshape(B, T, GLA_HEADS, GLA_DV).astype(f32))
    o_gla = o.reshape(B, T, GLA_WIDTH).astype(x.dtype)
    qs = _rope(sq.reshape(B, T, SWA_HEADS, SWA_HEAD_DIM), pos)
    ks = _rope(sk.reshape(B, T, SWA_KV_HEADS, SWA_HEAD_DIM), pos)
    vs = sv.reshape(B, T, SWA_KV_HEADS, SWA_HEAD_DIM)
    o_swa, kc, vc = attend(qs, ks, vs, sinks)
    x = x + jnp.concatenate([o_gla, o_swa.astype(x.dtype)], axis=-1) @ w_o
    h = _rmsnorm(x, norm_ffn)
    x = x + (jax.nn.silu(h @ w_gate) * (h @ w_up)) @ w_down
    return x, S, kc, vc

def setup_inputs(seed: int = 0) -> dict:
    key = jax.random.key(seed)
    ks = jax.random.split(key, 20)
    nrm = jax.random.normal
    w_buf = min(WINDOW, PAST_LEN)
    return {
        "x_prompt": nrm(ks[0], (BATCH, SEQ, D_MODEL), jnp.float32),
        "x_sample": nrm(ks[1], (DEC_BATCH, DEC_SEQ, D_MODEL), jnp.float32),
        "state_gla": 0.5 * nrm(ks[2], (DEPTH, DEC_BATCH, GLA_HEADS, GLA_DK, GLA_DV), jnp.float32),
        "cache_swa_k": nrm(ks[3], (DEPTH, DEC_BATCH, w_buf, SWA_KV_HEADS, SWA_HEAD_DIM), jnp.float32),
        "cache_swa_v": nrm(ks[4], (DEPTH, DEC_BATCH, w_buf, SWA_KV_HEADS, SWA_HEAD_DIM), jnp.float32),
        "norm_attn": 1.0 + 0.01 * nrm(ks[5], (DEPTH, D_MODEL), jnp.float32),
        "w_in": nrm(ks[6], (DEPTH, D_MODEL, IN_COLS), jnp.float32) * D_MODEL ** -0.5,
        "w_gk2": nrm(ks[7], (DEPTH, GATE_RANK, GLA_QK), jnp.float32) * GATE_RANK ** -0.5,
        "b_gk2": 0.1 * nrm(ks[8], (DEPTH, GLA_QK), jnp.float32),
        "gla_norm": 1.0 + 0.01 * nrm(ks[9], (DEPTH, GLA_DV), jnp.float32),
        "attn_sinks": 0.5 * nrm(ks[10], (DEPTH, SWA_HEADS), jnp.float32),
        "w_o": nrm(ks[11], (DEPTH, MIX_WIDTH, D_MODEL), jnp.float32) * MIX_WIDTH ** -0.5,
        "norm_ffn": 1.0 + 0.01 * nrm(ks[12], (DEPTH, D_MODEL), jnp.float32),
        "w_gate": nrm(ks[13], (DEPTH, D_MODEL, D_FF), jnp.float32) * D_MODEL ** -0.5,
        "w_up": nrm(ks[14], (DEPTH, D_MODEL, D_FF), jnp.float32) * D_MODEL ** -0.5,
        "w_down": nrm(ks[15], (DEPTH, D_FF, D_MODEL), jnp.float32) * D_FF ** -0.5,
        "norm_final": 1.0 + 0.01 * nrm(ks[16], (D_MODEL,), jnp.float32),
    }

def reference(x_prompt, x_sample, state_gla, cache_swa_k, cache_swa_v, norm_attn, w_in, w_gk2,
              b_gk2, gla_norm, attn_sinks, w_o, norm_ffn, w_gate, w_up, w_down, norm_final):
    pos_p = jnp.arange(x_prompt.shape[1])
    pos_s = PAST_LEN + jnp.arange(x_sample.shape[1])
    yp, ys = x_prompt, x_sample
    Sp_l, kp_l, vp_l, Ss_l, ks_l, vs_l = [], [], [], [], [], []
    for l in range(DEPTH):
        w = (norm_attn[l], w_in[l], w_gk2[l], b_gk2[l], gla_norm[l], attn_sinks[l], w_o[l],
             norm_ffn[l], w_gate[l], w_up[l], w_down[l])
        S0 = jnp.zeros((yp.shape[0], GLA_HEADS, GLA_DK, GLA_DV), jnp.float32)
        yp, Sp, kp, vp = _layer(yp, pos_p, S0, _swa_prompt, *w)
        attend_s = functools.partial(_swa_sample, kbuf=cache_swa_k[l], vbuf=cache_swa_v[l])
        ys, Ss, kss, vss = _layer(ys, pos_s, state_gla[l], attend_s, *w)
        Sp_l.append(Sp.astype(state_gla.dtype)); kp_l.append(kp.astype(cache_swa_k.dtype))
        vp_l.append(vp.astype(cache_swa_v.dtype)); Ss_l.append(Ss.astype(state_gla.dtype))
        ks_l.append(kss.astype(cache_swa_k.dtype)); vs_l.append(vss.astype(cache_swa_v.dtype))
    y_prompt = _rmsnorm(yp, norm_final)
    y_sample = _rmsnorm(ys, norm_final)
    return (y_prompt, y_sample, jnp.stack(Sp_l), jnp.stack(kp_l), jnp.stack(vp_l),
            jnp.stack(Ss_l), jnp.stack(ks_l), jnp.stack(vs_l))


_drawn_inputs = setup_inputs


def setup_inputs(seed=0):
    import zlib

    import numpy as np

    out = dict(_drawn_inputs(seed))
    spreads = {}
    factors = {'norm_attn': 3.258,
     'gla_norm': 8.0,
     'attn_sinks': 64.0,
     'norm_ffn': 5.215,
     'norm_final': 32.713}
    for name, (base, spread) in spreads.items():
        noise = np.random.default_rng([zlib.crc32(name.encode()), seed]).standard_normal(out[name].shape)
        drawn = base * np.exp(spread * noise) if base else spread * noise
        out[name] = __import__('jax').numpy.asarray(drawn.astype(out[name].dtype))
    for name, factor in factors.items():
        out[name] = (out[name] * factor).astype(out[name].dtype)
    return out
```

```python
import concourse.bass as bass
from concourse import mybir

D_MODEL = 1024
DEPTH = 2
SEQ = 1024
NB, NT = 8, 4
NS = NB * NT
T = SEQ + NS
P = 128
KC = D_MODEL // P
D_FF = 2816
FT = D_FF // P
FPAIRS = FT // 2
COLS = ((0, 384), (384, 768), (768, T))
NTT = len(COLS)
TW = 384
NCH = SEQ // P
GH = 4
PAIRS = GH // 2
SUB = 32
NSUB = P // SUB
WCACHE = 128
EPS = 1e-6
GATE_NORM = 16.0
CLAMP = 80.0 * GATE_NORM
UNIT = KC * P
RING = 2
ACCS = 3
NEG = -1.0e30

U_SK, U_SV, U_SQ, U_GK, U_GQ, U_GA, U_GV, U_GG, U_WO = 0, 1, 2, 6, 8, 10, 11, 15, 19
U_FF = 27
UNITS = U_FF + 6 * FPAIRS
FF_UNITS = 6
FF_GROUPS = 4 * NTT + KC * NTT

CONSTS = {"ident": 128, "ones": 128, "band": 256, "reset": 32, "bmask": NB,
          "causal": 128, "causal_s": 32, "eps": 1}
PARAMS = {"g_attn": KC, "g_ffn": KC, "g_gla": 1, "b_gate": PAIRS, "sink": 8, "sink_rows": 2}


def offsets(table):
    at, out = 0, {}
    for name, n in table.items():
        out[name] = (at, at + n)
        at += n
    return out, at


def schedule():
    steps = []
    for tt in range(NTT):
        steps += [("square", 0, tt), ("stat", 0, tt), ("normed", 0, tt)]
    held = []
    for u in range(U_SK, U_GK):
        for tt in range(NTT):
            steps += [("z", u, tt)] + held
            held = [("turn_v", u, tt)] if u == U_SV else []
    steps.append(("turn_k",))
    for g in range(2):
        steps += [("dec_scores", g), ("dec_norm", g), ("dec_turn", g), ("dec_values", g)]
    rest = []
    for u in range(U_GK, U_GG):
        for tt in range(NTT):
            rest.append([("z", u, tt)] + held)
            held = [("turn_v", u, tt)] if u >= U_GV else []
            if u == U_GA:
                held = [("gate", p, tt) for p in range(PAIRS)]
    rest.append(held)
    items = 2 * NCH
    done = 0
    for n in range(items + 1):
        if n < items:
            steps.append(("scores", n))
        upto = len(rest) * (n + 1) // (items + 1)
        half = done + (upto - done + 1) // 2
        for r in rest[done:half]:
            steps += r
        if n > 0:
            steps += [("turn_p", n - 1)]
        for r in rest[half:upto]:
            steps += r
        done = upto
        if n > 0:
            steps.append(("values", n - 1))
        if n < items:
            steps.append(("norm_p", n))
    steps.append(("gla_decays", 0))
    for c in range(NCH):
        steps.append(("gla_scores", c))
        if c + 1 < NCH:
            steps.append(("gla_decays", c + 1))
        steps += [("gla_state", c), ("gla_out", c), ("gla_state_sum", c)]
    steps.append(("gla_sample",))
    steps += [("gla_norm", c) for c in range(NCH + 1)]
    steps += [("z", u, tt) for u in range(U_GG, U_WO) for tt in range(NTT)]
    steps += [("split_out", tt) for tt in range(NTT)]
    steps += [("z", u, tt) for u in range(U_WO, U_FF) for tt in range(NTT)]
    for tt in range(NTT):
        steps += [("square", 1, tt), ("stat", 1, tt), ("normed", 1, tt)]
    return steps


GROUP_STEPS = ("z", "stat", "turn_v", "turn_k", "gate", "gla_norm")


def group_numbers(steps):
    table, n = {}, 0
    for s in steps:
        if s[0] in GROUP_STEPS:
            table[s] = n
            n += 1
    return table, n


def count_before(steps, kind, step):
    n = 0
    for s in steps:
        if s == step:
            return n
        n += s[0] == kind
    raise ValueError(step)


def trunk(nc, x_t, units, consts, tables, dec_mask, params, w_gk2, state_in, kcache_t,
          kcache, vcache, norm_final, y_t, state_p, kc_p, vc_p, state_s, kc_s, vc_s):
    f32, f32r, u32 = mybir.dt.float32, mybir.dt.float32r, mybir.dt.uint32
    ALU = mybir.AluOpType
    ACT = mybir.ActivationFunctionType
    AX = mybir.AxisListType
    STEPS = schedule()
    GROUP, G_FF = group_numbers(STEPS)
    CO, NCONST = offsets(CONSTS)
    PO, NPARAM = offsets(PARAMS)

    base = (nc.sbuf_base + 31) // 32 * 32
    top = [base]

    def region(nbytes):
        at = top[0]
        top[0] += (nbytes + 31) // 32 * 32
        return at

    def at(name, offset, shape, dt=f32):
        return nc.alloc_sbuf_tensor_at(name, shape, dt, offset=offset)

    x = at("x", region(KC * T * 4), [P, KC, T])
    h_hi = at("h_hi", region(KC * T * 4), [P, KC, T], f32r)
    h_lo = at("h_lo", region(KC * T * 4), [P, KC, T], f32r)
    w_raw = at("w_raw", region(RING * UNIT * 4), [P, RING, UNIT])
    w_hi = at("w_hi", region(RING * UNIT * 4), [P, RING, UNIT], f32r)
    w_lo = at("w_lo", region(RING * UNIT * 4), [P, RING, UNIT], f32r)
    const = at("const", region(NCONST * 4), [P, NCONST])
    par = at("par", region((NPARAM + KC + 10) * 4), [P, NPARAM + KC + 10])
    gfin = par[:, NPARAM:NPARAM + KC]
    nsink = par[:, NPARAM + KC:NPARAM + KC + 10]
    r_qs, r_ks, r_sv = region(4 * T * 4), region(T * 4), region(9 * P * 4)
    qs = at("qs", r_qs, [P, 4, T])
    ks = at("ks", r_ks, [P, T])
    sv = at("sv", r_sv, [P, 9, P])
    s0 = at("s0", r_ks, [P, NB, PAIRS, P])
    r_qg, r_kg, r_bg, r_vo = (region(PAIRS * T * 4), region(PAIRS * T * 4),
                              region(PAIRS * T * 4), region(9 * GH * P * 4))
    qg = at("qg", r_qg, [P, PAIRS, T])
    kg = at("kg", r_kg, [P, PAIRS, T])
    bg = at("bg", r_bg, [P, PAIRS, T])
    vo = at("vo", r_vo, [P, 9, GH, P])
    rope = at("rope", r_bg, [P, 2, T])
    dmask = at("dmask", r_vo, [P, T])
    kct = at("kct", r_vo + T * 4, [P, NB, WCACHE])
    vct = at("vct", r_vo + T * 4 + NB * WCACHE * 4, [P, NB, P])
    r_spare = r_vo + (T + 2 * NB * WCACHE) * 4
    gk2 = at("gk2", r_spare, [16, PAIRS * P])
    kno = at("kno", r_spare + 1024, [P, 2, P])
    dnew_t = at("dnew_t", r_spare + 2048, [NS, P])
    dq = at("dq", r_spare + 2560, [P, 4 * NS])
    r_big = region(3 * 4 * 256 * 4)
    prob = at("prob", r_big, [P, 2, 4, 256])
    prob_t = at("prob_t", r_big + 2 * 4 * 256 * 4, [P, 2, 4, P])
    dprob = at("dprob", r_big, [P, T])
    dprob_t = at("dprob_t", r_big + 2 * 4 * 256 * 4, [P, NB, P])
    edec = at("edec", r_big, [P, 2, 6 * 256])
    kdm = at("kdm", r_big + 4096, [NS, NB, PAIRS * P])
    esam = at("esam", r_big, [P, 2, 2, NS])
    r_t = region(4 * TW * 4)
    tmp_a = at("tmp_a", r_t, [P, 2, TW])
    tmp_b = at("tmp_b", r_t + 2 * TW * 4, [P, 2, TW])
    rstd = at("rstd", region(TW * 4), [P, TW])
    sqt = at("sqt", region(2 * TW * 4), [P, 2, TW])
    r_sum = region(2 * TW * 4)
    ssum = at("ssum", r_sum, [P, 2, TW])
    gat = at("gat", r_sum, [16, 2, TW])
    gsq = at("gsq", r_kg, [P, 2, GH * P])
    grstd = at("grstd", r_qg, [P, GH * P])
    o_s = at("o_s", r_qg + T * 4, [P, GH, NS])
    small = at("small", region(52 * 4), [P, 52])
    qh = at("qh", r_t + 2 * TW * 4, [P, 2, PAIRS, P])
    kdn = at("kdn", r_t, [P, 2, PAIRS, P])
    asb = at("asb", region(2 * GH * P * 4), [P, 2, GH, P])
    asam = at("asam", r_big + 2048, [NS, GH, NS])
    st = at("st", r_sum, [P, GH, P])
    hid_hi = at("hid_hi", r_qs, [P, 2, T], f32r)
    hid_lo = at("hid_lo", r_qs + 2 * T * 4, [P, 2, T], f32r)
    silu_g = at("silu_g", r_qg, [P, NTT, TW])
    assert top[0] <= nc.sbuf_usable_end, (top[0], nc.sbuf_usable_end)

    acc = [nc.alloc_psum_tensor(f"acc{b}", [P, 512], f32) for b in range(ACCS)]
    pair_a = nc.alloc_psum_tensor("pair_a", [P, 1024], f32)
    pair_b = nc.alloc_psum_tensor("pair_b", [P, 1024], f32)
    single = nc.alloc_psum_tensor("single", [P, 512], f32)

    def sem(name):
        return nc.alloc_semaphore(name)

    set_up = sem("set_up")
    zeroed = sem("zeroed")
    stored = sem("stored")
    fin = {n: sem(f"fin_{n}") for n in ("square", "added", "full", "ln", "rstd", "out", "stored")}
    acc_full = sem("acc_full")
    acc_free = [sem(f"acc_free{b}") for b in range(ACCS)]
    w_loaded = [sem(f"w_loaded{s}") for s in range(RING)]
    w_high = sem("w_high")
    w_ready = sem("w_ready")
    par_loaded = sem("par_loaded")
    loaded = sem("loaded")
    s0_loaded = sem("s0_loaded")
    out_sem = sem("out_sem")
    dve_chain = sem("dve_chain")
    act_chain = sem("act_chain")
    squares = sem("squares")
    sq_added = sem("sq_added")
    rstd_ready = sem("rstd_ready")
    hf_made = sem("hf_made")
    hi_made = sem("hi_made")
    h_ready = sem("h_ready")
    roped = sem("roped")
    gate_log = sem("gate_log")
    gates_ready = sem("gates_ready")
    dq_packed = sem("dq_packed")
    sc_full = sem("sc_full")
    sc_read = sem("sc_read")
    max_ready = sem("max_ready")
    p_exp = sem("p_exp")
    p_norm = sem("p_norm")
    pt_full = sem("pt_full")
    pt_copied = sem("pt_copied")
    pv_full = sem("pv_full")
    pv_copied = sem("pv_copied")
    dec_ready = sem("dec_ready")
    dec_exp = sem("dec_exp")
    dec_mult = sem("dec_mult")
    ga_full = sem("ga_full")
    ga_masked = sem("ga_masked")
    kd_turned = sem("kd_turned")
    kd_copied = sem("kd_copied")
    ds_full = sem("ds_full")
    s_ready = sem("s_ready")
    go_full = sem("go_full")
    go_copied = sem("go_copied")
    gn_square = sem("gn_square")
    gn_rstd = sem("gn_rstd")
    gn_done = sem("gn_done")
    sg_used = sem("sg_used")
    o_high = sem("o_high")
    o_ready = sem("o_ready")
    hid_high = sem("hid_high")
    hid_ready = sem("hid_ready")
    layer_sems = range(acc_full.num, hid_ready.num + 1)

    def c_(name, rows=P):
        a, b = CO[name]
        return const[0:rows, a:b]

    def p_(name, i=None, n=1):
        a, b = PO[name]
        return par[:, a:b] if i is None else par[:, a + i:a + i + n]

    def bank(g):
        return acc[g % ACCS]

    def left(eng, g):
        eng.wait_ge(acc_free[g % ACCS], g // ACCS + 1)

    def width(tt):
        return COLS[tt][1] - COLS[tt][0]

    def cols(tt):
        return slice(*COLS[tt])

    with nc.Block() as block:
        @block.sync
        def _(sp):
            sp.dma_start(const[:], consts).then_inc(set_up, 16)
            sp.dma_start(gfin, norm_final).then_inc(set_up, 16)
            for tt in range(NTT):
                sp.dma_start(x[:, :, cols(tt)], x_t[:, :, cols(tt)]).then_inc(set_up, 16)
            sp.wait_ge(set_up, 16 * (2 + NTT))

        @block.vector
        def _(dve):
            nc.vector.memset(asb[:], 0.0).then_inc(zeroed, 1)
            dve.wait_ge(zeroed, 1)

    with nc.Fori(0, DEPTH) as layer:
        with nc.Block() as block:

            @block.sync
            def _(sp):
                for u in range(U_FF):
                    if u >= RING:
                        sp.wait_ge(w_ready, u - RING + 1)
                    sp.dma_start(w_raw[:, u % RING, :], units[layer, u]).then_inc(w_loaded[u % RING], 16)
                with sp.Fori(0, FPAIRS) as i:
                    for j in range(FF_UNITS):
                        u = U_FF + j
                        sp.wait_ge(w_ready, i * FF_UNITS + (u - RING + 1))
                        sp.dma_start(w_raw[:, u % RING, :],
                                     units[layer, i * FF_UNITS + u]).then_inc(w_loaded[u % RING], 16)

            @block.gpsimd
            def _(pool):
                def split(u, loads, high, freed):
                    s = u % RING
                    if freed is not None:
                        pool.wait_ge(acc_full, freed)
                    pool.wait_ge(w_loaded[s], loads)
                    nc.gpsimd.tensor_tensor(w_hi[:, s, 0:SUB], w_raw[:, s, 0:SUB], c_("ones")[:, 0:SUB],
                                            ALU.mult)
                    nc.gpsimd.tensor_scalar(w_hi[:, s, SUB:], w_raw[:, s, SUB:], 1.0, 0.0,
                                            ALU.mult, ALU.add).then_inc(w_high, 1)
                    pool.wait_ge(w_high, high)
                    nc.gpsimd.tensor_tensor(w_lo[:, s, :], w_raw[:, s, :], w_hi[:, s, :].bitcast(f32),
                                            ALU.subtract).then_inc(w_ready, 1)

                for u in range(U_FF):
                    split(u, 16 * (u // RING + 1), u + 1,
                          GROUP[("z", u - RING, NTT - 1)] + 1 if u >= RING else None)
                ends = [NTT * (j + 1) for j in range(4)] + [4 * NTT + 4 * NTT * (j + 1) for j in range(2)]
                before = [ends[4] - FF_GROUPS, ends[5] - FF_GROUPS] + ends[0:4]
                for j in range(FF_UNITS):
                    u = U_FF + j
                    freed = GROUP[("z", u - RING, NTT - 1)] + 1 if j < RING else G_FF + before[j]
                    split(u, 16 * (u // RING + 1), u + 1, freed)
                with pool.Fori(1, FPAIRS) as i:
                    for j in range(FF_UNITS):
                        u = U_FF + j
                        split(u, i * (16 * FF_UNITS // RING) + 16 * (u // RING + 1),
                              i * FF_UNITS + (u + 1), i * FF_GROUPS + (G_FF + before[j]))

            @block.tensor
            def _(pe):
                def open_group(g):
                    if g >= ACCS:
                        pe.wait_ge(acc_free[g % ACCS], g // ACCS)

                def passes(out, slot, k, hi, lo, first, last):
                    wh = w_hi[:, slot, k * P:(k + 1) * P]
                    wl = w_lo[:, slot, k * P:(k + 1) * P]
                    nc.tensor.matmul(out, wh, hi, start=first, stop=False)
                    nc.tensor.matmul(out, wh, lo, start=False, stop=False)
                    return nc.tensor.matmul(out, wl, hi, start=False, stop=last)

                for s in STEPS:
                    if s[0] == "stat":
                        _, n, tt = s
                        g = GROUP[s]
                        open_group(g)
                        pe.wait_ge(sq_added, (KC - 1) * (NTT * n + tt + 1))
                        nc.tensor.matmul(bank(g)[:, 0:width(tt)], c_("ones"), ssum[:, tt % 2, 0:width(tt)],
                                         start=True, stop=True).then_inc(acc_full, 1)
                    elif s[0] == "z":
                        _, u, tt = s
                        g = GROUP[s]
                        open_group(g)
                        if tt == 0:
                            pe.wait_ge(w_ready, u + 1)
                        out = bank(g)[:, 0:width(tt)]
                        for k in range(KC):
                            if u == 0:
                                pe.wait_ge(h_ready, KC * tt + k + 1)
                            if u == U_WO:
                                pe.wait_ge(o_ready, KC * tt + k + 1)
                            last = passes(out, u % RING, k, h_hi[:, k, cols(tt)], h_lo[:, k, cols(tt)],
                                          k == 0, k == KC - 1)
                        last.then_inc(acc_full, 1)
                    elif s[0] == "turn_v":
                        _, u, tt = s
                        g = GROUP[s]
                        open_group(g)
                        left(pe, GROUP[("z", u, tt)])
                        n_done = count_before(STEPS, "turn_v", s)
                        for j in range(3):
                            w = NS if tt == NTT - 1 and j == 2 else P
                            last = nc.tensor.transpose(bank(g)[0:w, j * P:(j + 1) * P],
                                                       tmp_a[:, n_done % 2, j * P:j * P + w], c_("ident"))
                        last.then_inc(acc_full, 1)
                    elif s[0] == "turn_k":
                        g = GROUP[s]
                        open_group(g)
                        pe.wait_ge(roped, NTT)
                        nc.tensor.transpose(bank(g)[:, 0:P], ks[:, SEQ - P:SEQ], c_("ident"))
                        nc.tensor.transpose(bank(g)[0:NS, P:2 * P], ks[:, SEQ:T],
                                            c_("ident")).then_inc(acc_full, 1)
                    elif s[0] == "gate":
                        _, p, tt = s
                        g = GROUP[s]
                        open_group(g)
                        left(pe, GROUP[("z", U_GA, tt)])
                        pe.wait_ge(par_loaded, 32)
                        nc.tensor.matmul(bank(g)[:, 0:width(tt)], gk2[:, p * P:(p + 1) * P],
                                         gat[:, tt % 2, 0:width(tt)], start=True, stop=True).then_inc(acc_full, 1)
                    elif s[0] == "dec_scores":
                        _, g = s
                        r = slice(64 * g, 64 * g + 64)
                        if g == 0:
                            pe.wait_ge(dq_packed, 1)
                            pe.wait_ge(loaded, 16 * 4)
                        else:
                            pe.wait_ge(sc_read, g)
                            pe.wait_ge(pv_copied, g)
                        q = dq[r, :]
                        for b in range(2):
                            nc.tensor.matmul(pair_a[:, 512 * b:512 * b + 512], q, kct[r, 4 * b:4 * b + 4, :],
                                             start=True, stop=True)
                        nc.tensor.matmul(single[:, 0:NS], q, ks[r, SEQ:T], start=True,
                                         stop=True).then_inc(sc_full, 1)
                    elif s[0] == "dec_turn":
                        _, g = s
                        pe.wait_ge(p_norm, g + 1)
                        if g > 0:
                            pe.wait_ge(pt_copied, g)
                        for b in range(NB):
                            nc.tensor.transpose(pair_b[:, P * b:P * b + P], dprob[:, P * b:P * b + P], c_("ident"))
                        nc.tensor.transpose(single[0:NS, P:2 * P], dprob[:, SEQ:T],
                                            c_("ident")).then_inc(pt_full, 1)
                    elif s[0] == "dec_values":
                        _, g = s
                        r = slice(64 * g, 64 * g + 64)
                        pe.wait_ge(pt_copied, g + 1)
                        left(pe, GROUP[("turn_v", U_SV, NTT - 1)])
                        for b in range(NB):
                            nc.tensor.matmul(single[r, 256:384], vct[:, b, r], dprob_t[:, b, :],
                                             start=b == 0, stop=False)
                        nc.tensor.matmul(single[r, 256:384], sv[0:NS, 8, r], dnew_t[:, :],
                                         start=False, stop=True).then_inc(pv_full, 1)
                    elif s[0] == "scores":
                        n = s[1]
                        blk, g = n // 2, n % 2
                        r = slice(64 * g, 64 * g + 64)
                        lo = P if blk == 0 else 0
                        pe.wait_ge(sc_read, n + 2)
                        for hh in range(4):
                            last = nc.tensor.matmul(pair_a[:, 256 * hh + lo:256 * hh + 256],
                                                    qs[r, hh, blk * P:(blk + 1) * P],
                                                    ks[r, (blk - 1) * P + lo:(blk + 1) * P],
                                                    start=True, stop=True)
                        last.then_inc(sc_full, 1)
                    elif s[0] == "turn_p":
                        n = s[1]
                        blk = n // 2
                        pe.wait_ge(p_norm, n + 3)
                        pe.wait_ge(pt_copied, n + 2)
                        for kb in range(1 if blk == 0 else 0, 2):
                            for hh in range(4):
                                last = nc.tensor.transpose(pair_b[:, 512 * kb + P * hh:512 * kb + P * hh + P],
                                                           prob[:, n % 2, hh, P * kb:P * kb + P], c_("ident"))
                        last.then_inc(pt_full, 1)
                    elif s[0] == "values":
                        n = s[1]
                        blk, g = n // 2, n % 2
                        r = slice(64 * g, 64 * g + 64)
                        pe.wait_ge(pt_copied, n + 3)
                        pe.wait_ge(pv_copied, n + 2)
                        for kb in range(1 if blk == 0 else 0, 2):
                            last = nc.tensor.matmul(single[r, :], sv[:, blk - 1 + kb, r], prob_t[:, kb, :, :],
                                                    start=kb == (1 if blk == 0 else 0), stop=kb == 1)
                        last.then_inc(pv_full, 1)
                    elif s[0] == "gla_scores":
                        c = s[1]
                        pe.wait_ge(dec_mult, c + 1)
                        if c == 0:
                            pe.wait_ge(sc_read, 2 * NCH + 2)
                        else:
                            pe.wait_ge(ga_masked, c)
                        for hd in range(GH):
                            p, r = hd // 2, slice(64 * (hd % 2), 64 * (hd % 2) + 64)
                            for i in range(NSUB):
                                a = (p * NSUB + i) * P
                                q = 1024 + p * P + i * SUB
                                o = 512 * (hd % 2) + p * P + i * SUB
                                last = nc.tensor.matmul(pair_a[:, o:o + SUB], edec[r, c % 2, a:a + P],
                                                        edec[r, c % 2, q:q + SUB], start=True, stop=True)
                        last.then_inc(ga_full, 1)
                    elif s[0] == "gla_state":
                        c = s[1]
                        if c == 0:
                            pe.wait_ge(pt_copied, 2 * NCH + 2)
                            left(pe, GROUP[("turn_v", U_GG - 1, NTT - 1)])
                        else:
                            pe.wait_ge(kd_copied, c)
                        for p in range(PAIRS):
                            a = 1280 + p * P
                            last = nc.tensor.transpose(pair_b[:, p * P:(p + 1) * P], edec[:, c % 2, a:a + P],
                                                       c_("ident"))
                        last.then_inc(kd_turned, 1)
                        pe.wait_ge(kd_copied, c + 1)
                        if c > 0:
                            pe.wait_ge(s_ready, c)
                        for hd in range(GH):
                            p, r = hd // 2, slice(64 * (hd % 2), 64 * (hd % 2) + 64)
                            last = nc.tensor.matmul(pair_b[r, 512 + p * P:512 + (p + 1) * P],
                                                    kdn[:, c % 2, p, r], vo[:, c, hd, :], start=True, stop=True)
                        last.then_inc(ds_full, 1)
                    elif s[0] == "gla_out":
                        c = s[1]
                        pe.wait_ge(ga_masked, c + 1)
                        if c == 0:
                            pe.wait_ge(pv_copied, 2 * NCH + 2)
                        else:
                            pe.wait_ge(go_copied, c)
                            pe.wait_ge(s_ready, c)
                        for hd in range(GH):
                            last = nc.tensor.matmul(single[:, hd * P:(hd + 1) * P], vo[:, c, hd, :],
                                                    asb[:, c % 2, hd, :], start=True, stop=c == 0)
                            if c > 0:
                                last = nc.tensor.matmul(single[:, hd * P:(hd + 1) * P], st[:, hd, :],
                                                        qh[:, c % 2, hd // 2, :], start=False, stop=True)
                        last.then_inc(go_full, 1)
                    elif s[0] == "gla_norm":
                        c = s[1]
                        g = GROUP[s]
                        open_group(g)
                        w = P if c < NCH else NS
                        pe.wait_ge(gn_square, c + 1)
                        nc.tensor.matmul(bank(g)[:, 0:GH * w], c_("ones"), gsq[:, c % 2, 0:GH * w],
                                         start=True, stop=True).then_inc(acc_full, 1)
                    elif s[0] == "gla_sample":
                        pe.wait_ge(dec_mult, NCH + 1)
                        pe.wait_ge(ga_masked, NCH)
                        for hd in range(GH):
                            p, r = hd // 2, slice(64 * (hd % 2), 64 * (hd % 2) + 64)
                            last = nc.tensor.matmul(pair_a[0:NS, 512 * (hd % 2) + p * NS:512 * (hd % 2) + (p + 1) * NS], esam[r, 0, p, :],
                                                    qh[r, 0, p, 0:NS], start=True, stop=True)
                        last.then_inc(ga_full, 1)
                        pe.wait_ge(s_ready, NCH)
                        for p in range(PAIRS):
                            last = nc.tensor.transpose(pair_b[0:NS, p * P:(p + 1) * P], esam[:, 1, p, :],
                                                       c_("ident"))
                        last.then_inc(kd_turned, 1)
                        pe.wait_ge(ga_masked, NCH + 1)
                        pe.wait_ge(go_copied, NCH)
                        pe.wait_ge(s0_loaded, 32)
                        for hd in range(GH):
                            p, r = hd // 2, slice(64 * (hd % 2), 64 * (hd % 2) + 64)
                            bank_o = single if hd % 2 == 0 else pair_b[:, 512:1024]
                            o = p * NS
                            last = nc.tensor.matmul(bank_o[:, o:o + NS], vo[0:NS, NCH, hd, :], asam[:, hd, :],
                                                    start=True, stop=False, skip_group_check=True)
                            for b in range(NB):
                                last = nc.tensor.matmul(bank_o[:, o + NT * b:o + NT * (b + 1)], s0[r, b, p, :],
                                                        qh[r, 0, p, NT * b:NT * (b + 1)], start=False,
                                                        stop=b == NB - 1, skip_group_check=True)
                        last.then_inc(go_full, 1)
                        pe.wait_ge(kd_copied, NCH + 2)
                        pe.wait_ge(go_copied, NCH + 1)
                        for b in range(NB):
                            for hd in range(GH):
                                p, r = hd // 2, slice(64 * (hd % 2), 64 * (hd % 2) + 64)
                                dst = pair_a if b < 4 else pair_b
                                o = (b % 4) * 256 + p * P
                                last = nc.tensor.matmul(dst[r, o:o + P],
                                                        kdm[:, b, p * P + r.start:p * P + r.stop],
                                                        vo[0:NS, NCH, hd, :], start=True, stop=True)
                        last.then_inc(ds_full, 1)

                with pe.Fori(0, FPAIRS) as i:
                    def ff_open(j):
                        g = G_FF + j
                        pe.wait_ge(acc_free[g % ACCS], i * (FF_GROUPS // ACCS) + g // ACCS)
                        return bank(g)

                    for j in range(4):
                        u = U_FF + j
                        pe.wait_ge(w_ready, i * FF_UNITS + (u + 1))
                        for tt in range(NTT):
                            out = ff_open(NTT * j + tt)[:, 0:width(tt)]
                            for k in range(KC):
                                if j == 0:
                                    pe.wait_ge(h_ready, KC * (NTT + tt) + k + 1)
                                last = passes(out, u % RING, k, h_hi[:, k, cols(tt)], h_lo[:, k, cols(tt)],
                                              k == 0, k == KC - 1)
                            last.then_inc(acc_full, 1)
                    for j in range(2):
                        u = U_FF + 4 + j
                        pe.wait_ge(w_ready, i * FF_UNITS + (u + 1))
                        for tt in range(NTT):
                            pe.wait_ge(hid_ready, i * (2 * NTT) + (NTT + tt + 1))
                            for d in range(4):
                                out = ff_open(4 * NTT + 4 * (NTT * j + tt) + d)[:, 0:width(tt)]
                                for f in range(2):
                                    last = passes(out, u % RING, 4 * f + d, hid_hi[:, f, cols(tt)],
                                                  hid_lo[:, f, cols(tt)], f == 0, f == 1)
                                last.then_inc(acc_full, 1)

            @block.scalar
            def _(act):
                chain = [0]

                def link(ins):
                    chain[0] += 1
                    ins.then_inc(act_chain, 1)
                    act.wait_ge(act_chain, chain[0])

                act.dma_start(par[:, 0:NPARAM], params[layer]).then_inc(par_loaded, 16)
                act.dma_start(gk2[:], w_gk2[layer]).then_inc(par_loaded, 16)
                act.dma_start(rope[:], tables).then_inc(loaded, 16)
                act.dma_start(dmask[:], dec_mask).then_inc(loaded, 16)
                act.dma_start(kct[:], kcache_t[layer]).then_inc(loaded, 16)
                act.dma_start(vct[:], vcache[layer].rearrange("b t c -> t b c")).then_inc(loaded, 16)
                act.dma_start(kc_s[layer, :, 0:WCACHE - NT, :], kcache[layer, :, NT:WCACHE, :]).then_inc(out_sem, 16)
                act.dma_start(vc_s[layer, :, 0:WCACHE - NT, :], vcache[layer, :, NT:WCACHE, :]).then_inc(out_sem, 16)

                for s in STEPS:
                    if s[0] == "square":
                        _, n, tt = s
                        m = NTT * n + tt
                        w = width(tt)
                        if n == 1 and tt == 0:
                            act.wait_ge(out_sem, 16 * (5 + GH + 2 * NB))
                        for k in range(KC):
                            if n == 1:
                                left(act, GROUP[("z", U_WO + k, tt)])
                            if k == 0:
                                dst = ssum[:, tt % 2, 0:w]
                            else:
                                taken = (KC - 1) * m + max(k - 2, 0)
                                if taken > 0:
                                    act.wait_ge(sq_added, taken)
                                dst = sqt[:, k % 2, 0:w]
                            nc.scalar.activation(dst, x[:, k, cols(tt)], ACT.Square).then_inc(squares, 1)
                    elif s[0] == "stat":
                        _, n, tt = s
                        g = GROUP[s]
                        w = width(tt)
                        m = NTT * n + tt
                        act.wait_ge(acc_full, g + 1)
                        if m > 0:
                            act.wait_ge(hf_made, KC * m)
                        nc.scalar.activation(rstd[:, 0:w], bank(g)[:, 0:w], ACT.Ln, bias=c_("eps"),
                                             scale=1.0 / D_MODEL).then_inc(acc_free[g % ACCS], 1)
                        act.wait_ge(acc_free[g % ACCS], g // ACCS + 1)
                        nc.scalar.activation(rstd[:, 0:w], rstd[:, 0:w], ACT.Exp,
                                             scale=-0.5).then_inc(rstd_ready, 1)
                    elif s[0] == "normed":
                        _, n, tt = s
                        m = NTT * n + tt
                        if n == 1:
                            act.wait_ge(acc_full, GROUP[("z", U_FF - 1, tt)] + 1)
                        for k in range(KC):
                            act.wait_ge(hf_made, KC * m + k + 1)
                            nc.scalar.activation(h_hi[:, k, cols(tt)], tmp_a[:, k % 2, 0:width(tt)],
                                                 ACT.Copy).then_inc(hi_made, 1)
                    elif s[0] == "z":
                        _, u, tt = s
                        g = GROUP[s]
                        w = width(tt)
                        b = bank(g)
                        if u == U_SV or U_GV <= u < U_GG:
                            act.wait_ge(acc_full, g + 1)
                            n_done = count_before(STEPS, "turn_v", ("turn_v", u, tt))
                            if u == U_SV and tt < 2:
                                act.wait_ge(h_ready, KC * NTT)
                            nc.scalar.activation(tmp_a[:, n_done % 2, 0:w], b[:, 0:w], ACT.Copy)\
                              .then_inc(acc_free[g % ACCS], 1)
                        elif U_GK <= u < U_GA:
                            act.wait_ge(acc_full, g + 1)
                            dst = (kg if u < U_GQ else qg)[:, (u - U_GK) % 2, cols(tt)]
                            nc.scalar.activation(dst, b[:, 0:w], ACT.Copy, scale=1.0 if u < U_GQ else 0.125)\
                              .then_inc(acc_free[g % ACCS], 1)
                        elif u == U_GA:
                            act.wait_ge(acc_full, g + 1)
                            nc.scalar.activation(gat[:, tt % 2, 0:w], b[0:16, 0:w], ACT.Copy)\
                              .then_inc(acc_free[g % ACCS], 1)
                        elif U_GG <= u < U_WO:
                            act.wait_ge(acc_full, g + 1)
                            n_done = NTT * (u - U_GG) + tt
                            if n_done == 0:
                                act.wait_ge(gates_ready, PAIRS * NTT)
                            if n_done >= 2:
                                act.wait_ge(sg_used, n_done - 1)
                            nc.scalar.activation(tmp_b[:, n_done % 2, 0:w], b[:, 0:w], ACT.Silu)\
                              .then_inc(acc_free[g % ACCS], 1)
                    elif s[0] == "turn_v":
                        _, u, tt = s
                        g = GROUP[s]
                        act.wait_ge(acc_full, g + 1)
                        b3 = bank(g)[:, 0:3 * P].rearrange("p (j n) -> p j n", j=3)
                        nj = 3 if tt < NTT - 1 else 2
                        if u == U_SV:
                            dst, new = sv[:, 3 * tt:3 * tt + nj, :], sv[0:NS, 8, :]
                        else:
                            if u == U_GV and tt == 0:
                                act.wait_ge(pv_full, 2)
                                act.wait_ge(out_sem, 16 * (4 + 2 * NB))
                            hd = u - U_GV
                            dst, new = vo[:, 3 * tt:3 * tt + nj, hd, :], vo[0:NS, 8, hd, :]
                        last = nc.scalar.activation(dst, b3[:, 0:nj, :], ACT.Copy)
                        if tt == NTT - 1:
                            last = nc.scalar.activation(new, bank(g)[0:NS, 2 * P:3 * P], ACT.Copy)
                        last.then_inc(acc_free[g % ACCS], 1)
                    elif s[0] == "turn_k":
                        g = GROUP[s]
                        act.wait_ge(acc_full, g + 1)
                        nc.scalar.activation(kno[:, 0, :], bank(g)[:, 0:P], ACT.Copy)
                        nc.scalar.activation(kno[0:NS, 1, :], bank(g)[0:NS, P:2 * P], ACT.Copy)\
                          .then_inc(acc_free[g % ACCS], 1)
                        act.wait_ge(acc_free[g % ACCS], g // ACCS + 1)
                        act.dma_start(kc_p[layer, 0], kno[:, 0, :]).then_inc(out_sem, 16)
                        act.dma_start(vc_p[layer, 0], sv[:, NCH - 1, :]).then_inc(out_sem, 16)
                        for b in range(NB):
                            r = slice(NT * b, NT * (b + 1))
                            act.dma_start(kc_s[layer, b, WCACHE - NT:WCACHE, :], kno[r, 1, :]).then_inc(out_sem, 16)
                            act.dma_start(vc_s[layer, b, WCACHE - NT:WCACHE, :], sv[r, 8, :]).then_inc(out_sem, 16)
                    elif s[0] == "gate":
                        _, p, tt = s
                        g = GROUP[s]
                        w = width(tt)
                        n_done = PAIRS * tt + p
                        act.wait_ge(acc_full, g + 1)
                        if n_done > 0:
                            act.wait_ge(gates_ready, n_done)
                        else:
                            act.wait_ge(par_loaded, 32)
                            act.wait_ge(roped, 5 * NTT)
                        nc.scalar.activation(tmp_b[:, 0, 0:w], bank(g)[:, 0:w], ACT.Identity,
                                             bias=p_("b_gate", p)).then_inc(acc_free[g % ACCS], 1)
                        act.wait_ge(acc_free[g % ACCS], g // ACCS + 1)
                        link(nc.scalar.activation(tmp_b[:, 1, 0:w], tmp_b[:, 0, 0:w], ACT.Abs))
                        link(nc.scalar.activation(tmp_b[:, 1, 0:w], tmp_b[:, 1, 0:w], ACT.Exp, scale=-1.0))
                        nc.scalar.activation(tmp_b[:, 1, 0:w], tmp_b[:, 1, 0:w], ACT.Ln, bias=1.0)\
                          .then_inc(gate_log, 1)
                    elif s[0] in ("dec_scores", "scores"):
                        n = s[1]
                        if s[0] == "dec_scores":
                            act.wait_ge(max_ready, n + 1)
                            nc.scalar.activation(small[:, 3:4], small[:, 2:3], ACT.Exp)
                            nc.scalar.activation(dprob[:], dprob[:], ACT.Exp, bias=small[:, 1:2],
                                                 accum_out=small[:, 4:5]).then_inc(p_exp, 1)
                        else:
                            lo = P if n < 2 else 0
                            o = 24 * (n % 2)
                            act.wait_ge(max_ready, n + 3)
                            nc.scalar.activation(small[:, o + 12:o + 16], small[:, o + 8:o + 12], ACT.Exp)
                            for hh in range(4):
                                pr = prob[:, n % 2, hh, lo:256]
                                last = nc.scalar.activation(pr, pr, ACT.Exp, bias=small[:, o + 4 + hh:o + 5 + hh],
                                                            accum_out=small[:, o + 16 + hh:o + 17 + hh])
                            last.then_inc(p_exp, 1)
                    elif s[0] == "dec_turn":
                        _, g = s
                        act.wait_ge(pt_full, g + 1)
                        if g > 0:
                            act.wait_ge(pv_full, g)
                        nc.scalar.activation(dprob_t[:], pair_b[:].rearrange("p (b n) -> p b n", b=NB), ACT.Copy)
                        nc.scalar.activation(dnew_t[:], single[0:NS, P:2 * P], ACT.Copy).then_inc(pt_copied, 1)
                    elif s[0] == "turn_p":
                        n = s[1]
                        k0 = 1 if n < 2 else 0
                        act.wait_ge(pt_full, n + 3)
                        act.wait_ge(pv_full, n + 2)
                        nc.scalar.activation(prob_t[:, k0:2, :, :],
                                             pair_b[:, 512 * k0:1024].rearrange("p (a h n) -> p a h n", h=4, n=P),
                                             ACT.Copy).then_inc(pt_copied, 1)
                    elif s[0] in ("dec_values", "values"):
                        if s[0] == "dec_values":
                            g = s[1]
                            r = slice(64 * g, 64 * g + 64)
                            act.wait_ge(pv_full, g + 1)
                            nc.scalar.activation(qs[r, :, SEQ:T],
                                                 single[r, 256:384].rearrange("p (h n) -> p h n", h=4),
                                                 ACT.Copy).then_inc(pv_copied, 1)
                        else:
                            n = s[1]
                            blk, g = n // 2, n % 2
                            r = slice(64 * g, 64 * g + 64)
                            act.wait_ge(pv_full, n + 3)
                            nc.scalar.activation(qs[r, :, blk * P:(blk + 1) * P],
                                                 single[r, :].rearrange("p (h n) -> p h n", h=4),
                                                 ACT.Copy).then_inc(pv_copied, 1)
                            if n == 2 * NCH - 1:
                                act.wait_ge(out_sem, 16 * (4 + 2 * NB))
                                for b in range(0, NB, 4):
                                    act.dma_start(s0[:, b:b + 4], state_in[layer, b:b + 4].rearrange(
                                        "b (q r) v -> r b q v", r=P)).then_inc(s0_loaded, 16)
                    elif s[0] == "gla_decays":
                        c = s[1]
                        cc = slice(c * P, (c + 1) * P)
                        act.wait_ge(gates_ready, PAIRS * NTT)
                        if c >= 2:
                            act.wait_ge(s_ready, c - 1)
                            act.wait_ge(go_full, c - 1)
                        nc.scalar.activation(qh[:, c % 2, :, :], bg[:, :, cc], ACT.Exp, scale=1.0 / GATE_NORM)
                        act.wait_ge(dec_ready, c + 1)
                        nc.scalar.activation(edec[:, c % 2, :], edec[:, c % 2, :], ACT.Exp,
                                             scale=1.0 / GATE_NORM).then_inc(dec_exp, 1)
                    elif s[0] == "gla_state":
                        c = s[1]
                        act.wait_ge(kd_turned, c + 1)
                        nc.scalar.activation(kdn[:, c % 2, :, :],
                                             pair_b[:, 0:PAIRS * P].rearrange("p (q n) -> p q n", q=PAIRS),
                                             ACT.Copy).then_inc(kd_copied, 1)
                    elif s[0] == "gla_out":
                        c = s[1]
                        act.wait_ge(go_full, c + 1)
                        nc.scalar.activation(vo[:, c, :, :], single[:].rearrange("p (h n) -> p h n", h=GH),
                                             ACT.Copy).then_inc(go_copied, 1)
                    elif s[0] == "gla_state_sum":
                        if s[1] == NCH - 1:
                            act.wait_ge(s_ready, NCH)
                            for hd in range(GH):
                                r = slice(64 * (hd % 2), 64 * (hd % 2) + 64)
                                act.dma_start(state_p[layer, 0, 64 * hd:64 * hd + 64], st[r, hd, :])\
                                   .then_inc(out_sem, 16)
                    elif s[0] == "gla_norm":
                        c = s[1]
                        g = GROUP[s]
                        w = P if c < NCH else NS
                        act.wait_ge(go_copied, c + 1)
                        if c >= 2:
                            act.wait_ge(acc_full, GROUP[("gla_norm", c - 2)] + 1)
                        if c == 0:
                            act.wait_ge(dec_mult, NCH + 1)
                        sq3 = gsq[:, c % 2, 0:GH * w].rearrange("p (h n) -> p h n", h=GH)
                        nc.scalar.activation(sq3, vo[:, c, :, :] if c < NCH else o_s[:], ACT.Square).then_inc(gn_square, 1)
                        act.wait_ge(acc_full, g + 1)
                        if c > 0:
                            act.wait_ge(gn_done, c)
                        nc.scalar.activation(grstd[:, 0:GH * w], bank(g)[:, 0:GH * w], ACT.Ln, bias=c_("eps"),
                                             scale=1.0 / P).then_inc(acc_free[g % ACCS], 1)
                        act.wait_ge(acc_free[g % ACCS], g // ACCS + 1)
                        nc.scalar.activation(grstd[:, 0:GH * w], grstd[:, 0:GH * w], ACT.Exp,
                                             scale=-0.5).then_inc(gn_rstd, 1)
                    elif s[0] == "gla_sample":
                        act.wait_ge(go_full, NCH - 1)
                        nc.scalar.activation(qh[:, 0, :, 0:NS], bg[:, :, SEQ:T], ACT.Exp, scale=1.0 / GATE_NORM)
                        act.wait_ge(dec_ready, NCH + 1)
                        nc.scalar.activation(esam[:], esam[:], ACT.Exp, scale=1.0 / GATE_NORM).then_inc(dec_exp, 1)
                        act.wait_ge(kd_turned, NCH + 1)
                        nc.scalar.activation(kdn[0:NS, 0, :, :],
                                             pair_b[0:NS, 0:PAIRS * P].rearrange("p (q n) -> p q n", q=PAIRS),
                                             ACT.Copy).then_inc(kd_copied, 1)
                        act.wait_ge(go_full, NCH + 1)
                        for j, src in ((0, single[:, 0:PAIRS * NS]), (1, pair_b[:, 512:512 + PAIRS * NS])):
                            last = nc.scalar.activation(o_s[:, j:GH:2, :],
                                                        src.rearrange("p (h n) -> p h n", h=PAIRS), ACT.Copy)
                        last.then_inc(go_copied, 1)
                        act.wait_ge(s_ready, NCH + 1)
                        act.dma_start(state_s[layer].rearrange("b (q r) v -> r b q v", r=P), s0[:])\
                           .then_inc(out_sem, 16)
                    elif s[0] == "split_out":
                        tt = s[1]
                        act.wait_ge(acc_full, GROUP[("z", U_WO - 1, NTT - 1)] + 1)
                        nj = 3 if tt < NTT - 1 else 2
                        for k in range(KC):
                            c0 = COLS[tt][0]
                            if k < GH:
                                act.wait_ge(sg_used, NTT * k + tt + 1)
                                dst = h_hi[:, k, c0:c0 + nj * P].rearrange("p (j n) -> p j n", j=nj)
                                last = nc.scalar.activation(dst, vo[:, 3 * tt:3 * tt + nj, k, :], ACT.Copy)
                                if tt == NTT - 1:
                                    last = nc.scalar.activation(h_hi[:, k, SEQ:T], o_s[:, k, :], ACT.Copy)
                            else:
                                if k == GH and tt == 0:
                                    act.wait_ge(pv_copied, 2 * NCH + 2)
                                last = nc.scalar.activation(h_hi[:, k, cols(tt)], qs[:, k - GH, cols(tt)], ACT.Copy)
                            last.then_inc(o_high, 1)

                with act.Fori(0, FPAIRS) as i:
                    for f in range(2):
                        for tt in range(NTT):
                            w = width(tt)
                            j = 2 * NTT * f + tt
                            g = G_FF + j
                            n_done = NTT * f + tt
                            act.wait_ge(acc_full, i * FF_GROUPS + (g + 1))
                            nc.scalar.activation(silu_g[:, tt, 0:w], bank(g)[:, 0:w], ACT.Silu)\
                              .then_inc(acc_free[g % ACCS], 1)
                        for tt in range(NTT):
                            w = width(tt)
                            n_done = NTT * f + tt
                            g = G_FF + NTT * (2 * f + 1) + tt
                            act.wait_ge(acc_free[g % ACCS], i * (FF_GROUPS // ACCS) + (g // ACCS + 1))
                            nc.scalar.activation(hid_hi[:, f, cols(tt)], tmp_a[:, n_done % 2, 0:w],
                                                 ACT.Copy).then_inc(hid_high, 1)

            @block.vector
            def _(dve):
                chain = [0]

                def link(ins):
                    chain[0] += 1
                    ins.then_inc(dve_chain, 1)
                    dve.wait_ge(dve_chain, chain[0])

                dve.wait_ge(par_loaded, 32)
                a = PO["sink"][0]
                nc.vector.tensor_scalar(nsink, par[:, a:a + 10], -1.0, None, ALU.mult)
                for s in STEPS:
                    if s[0] == "square":
                        _, n, tt = s
                        m = NTT * n + tt
                        w = width(tt)
                        for k in range(1, KC):
                            dve.wait_ge(squares, KC * m + k + 1)
                            if k > 1:
                                dve.wait_ge(sq_added, (KC - 1) * m + k - 1)
                            nc.vector.tensor_tensor(ssum[:, tt % 2, 0:w], ssum[:, tt % 2, 0:w],
                                                    sqt[:, k % 2, 0:w], ALU.add).then_inc(sq_added, 1)
                    elif s[0] == "normed":
                        _, n, tt = s
                        m = NTT * n + tt
                        w = width(tt)
                        dve.wait_ge(rstd_ready, m + 1)
                        if n == 1:
                            dve.wait_ge(acc_full, GROUP[("z", U_FF - 1, tt)] + 1)
                        gain = "g_attn" if n == 0 else "g_ffn"
                        for k in range(KC + 1):
                            if k < KC:
                                if KC * m + k > 1:
                                    dve.wait_ge(h_ready, KC * m + k - 1)
                                nc.vector.scalar_tensor_tensor(
                                    tmp_a[:, k % 2, 0:w], x[:, k, cols(tt)], p_(gain, k), rstd[:, 0:w],
                                    ALU.mult, ALU.mult).then_inc(hf_made, 1)
                            if k > 0:
                                dve.wait_ge(hi_made, KC * m + k)
                                nc.vector.tensor_tensor(h_lo[:, k - 1, cols(tt)], tmp_a[:, (k - 1) % 2, 0:w],
                                                        h_hi[:, k - 1, cols(tt)].bitcast(f32),
                                                        ALU.subtract).then_inc(h_ready, 1)
                    elif s[0] == "z":
                        _, u, tt = s
                        g = GROUP[s]
                        w = width(tt)
                        b = bank(g)
                        if u == U_SK or U_SQ <= u < U_SQ + 4:
                            dst = ks[:, cols(tt)] if u == U_SK else qs[:, u - U_SQ, cols(tt)]
                            dve.wait_ge(acc_full, g + 1)
                            if u == U_SK and tt == 0:
                                dve.wait_ge(loaded, 16 * 4)
                            turn = tt if u == U_SK else NTT * (1 + u - U_SQ) + tt
                            if turn > 0:
                                dve.wait_ge(roped, turn)
                            for a in range(4):
                                o = 32 * (a ^ 1)
                                nc.vector.tensor_tensor(tmp_b[32 * a:32 * a + 32, 0, 0:w], b[o:o + 32, 0:w],
                                                        rope[32 * a:32 * a + 32, 1, cols(tt)], ALU.mult)
                            nc.vector.tensor_tensor(tmp_b[:, 1, 0:w], b[:, 0:w], rope[:, 0, cols(tt)],
                                                    ALU.mult).then_inc(acc_free[g % ACCS], 1)
                            dve.wait_ge(acc_free[g % ACCS], g // ACCS + 1)
                            nc.vector.tensor_tensor(dst, tmp_b[:, 0, 0:w], tmp_b[:, 1, 0:w],
                                                    ALU.add).then_inc(roped, 1)
                        elif U_GG <= u < U_WO:
                            hd = u - U_GG
                            n_done = NTT * hd + tt
                            left(dve, g)
                            if n_done == 0:
                                dve.wait_ge(gn_done, NCH + 1)
                            nj = 3 if tt < NTT - 1 else 2
                            sg = tmp_b[:, n_done % 2, 0:nj * P].rearrange("p (j n) -> p j n", j=nj)
                            o = vo[:, 3 * tt:3 * tt + nj, hd, :]
                            last = nc.vector.tensor_tensor(o, o, sg, ALU.mult)
                            if tt == NTT - 1:
                                o = o_s[:, hd, :]
                                last = nc.vector.tensor_tensor(o, o, tmp_b[:, n_done % 2, 2 * P:2 * P + NS], ALU.mult)
                            last.then_inc(sg_used, 1)
                        elif u >= U_WO:
                            dve.wait_ge(acc_full, g + 1)
                            xs = x[:, u - U_WO, cols(tt)]
                            nc.vector.tensor_tensor(xs, xs, b[:, 0:w], ALU.add).then_inc(acc_free[g % ACCS], 1)
                    elif s[0] == "gate":
                        _, p, tt = s
                        w = width(tt)
                        n_done = PAIRS * tt + p
                        dve.wait_ge(gate_log, n_done + 1)
                        link(nc.vector.scalar_tensor_tensor(tmp_b[:, 0, 0:w], tmp_b[:, 0, 0:w], 0.0,
                                                            tmp_b[:, 1, 0:w], ALU.min, ALU.subtract))
                        c0 = COLS[tt][0]
                        for j in range(3 if tt < NTT - 1 else 2):
                            last = nc.vector.tensor_tensor_scan(
                                bg[:, p, c0 + j * P:c0 + (j + 1) * P], c_("ones"),
                                tmp_b[:, 0, j * P:(j + 1) * P], 0.0, ALU.mult, ALU.add)
                        if tt == NTT - 1:
                            last = nc.vector.tensor_tensor_scan(bg[:, p, SEQ:T], c_("reset"),
                                                                tmp_b[:, 0, 2 * P:2 * P + NS], 0.0,
                                                                ALU.mult, ALU.add)
                        last.then_inc(gates_ready, 1)
                    elif s[0] == "dec_scores":
                        _, g = s
                        if g == 0:
                            dve.wait_ge(roped, 5 * NTT)
                            nc.vector.tensor_copy(dq[:].rearrange("p (h n) -> p h n", h=4),
                                                  qs[:, :, SEQ:T]).then_inc(dq_packed, 1)
                        dve.wait_ge(sc_full, g + 1)
                        if g > 0:
                            dve.wait_ge(pt_full, g)
                        nc.vector.scalar_tensor_tensor(dprob[:, 0:1024], pair_a[:], 0.125, dmask[:, 0:1024],
                                                       ALU.mult, ALU.add)
                        nc.vector.scalar_tensor_tensor(dprob[:, SEQ:T], single[:, 0:NS], 0.125, dmask[:, SEQ:T],
                                                       ALU.mult, ALU.add).then_inc(sc_read, 1)
                        dve.wait_ge(sc_read, g + 1)
                        link(nc.vector.tensor_reduce(small[:, 0:1], dprob[:], AX.X, ALU.max, negate=True))
                        link(nc.vector.tensor_tensor(small[:, 1:2], small[:, 0:1], nsink[:, 8 + g:9 + g], ALU.min))
                        nc.vector.tensor_tensor(small[:, 2:3], small[:, 1:2], p_("sink_rows", g),
                                                ALU.add).then_inc(max_ready, 1)
                    elif s[0] == "dec_norm":
                        _, g = s
                        dve.wait_ge(p_exp, g + 1)
                        link(nc.vector.tensor_tensor(small[:, 5:6], small[:, 3:4], small[:, 4:5], ALU.add))
                        link(nc.vector.reciprocal(small[:, 6:7], small[:, 5:6]))
                        nc.vector.tensor_scalar(dprob[:], dprob[:], small[:, 6:7], None, ALU.mult).then_inc(p_norm, 1)
                    elif s[0] == "scores":
                        n = s[1]
                        blk, g = n // 2, n % 2
                        lo = P if blk == 0 else 0
                        o = 24 * (n % 2)
                        pr = prob[:, n % 2, :, lo:256]
                        sc = pair_a[:].rearrange("p (h n) -> p h n", h=4)[:, :, lo:256]
                        band = c_("band")[:, lo:256].unsqueeze(1).broadcast_to([P, 4, 256 - lo])
                        dve.wait_ge(sc_full, n + 3)
                        dve.wait_ge(pt_full, max(n - 2 + 3, 2))
                        nc.vector.scalar_tensor_tensor(pr, sc, 0.125, band, ALU.mult, ALU.add).then_inc(sc_read, 1)
                        dve.wait_ge(sc_read, n + 3)
                        link(nc.vector.tensor_reduce(small[:, o:o + 4], pr, AX.X, ALU.max, negate=True))
                        link(nc.vector.tensor_tensor(small[:, o + 4:o + 8], small[:, o:o + 4],
                                                     nsink[:, 4 * g:4 * g + 4], ALU.min))
                        nc.vector.tensor_tensor(small[:, o + 8:o + 12], small[:, o + 4:o + 8],
                                                p_("sink", 4 * g, 4), ALU.add).then_inc(max_ready, 1)
                    elif s[0] == "norm_p":
                        n = s[1]
                        lo = P if n < 2 else 0
                        o = 24 * (n % 2)
                        pr = prob[:, n % 2, :, lo:256]
                        dve.wait_ge(p_exp, n + 3)
                        link(nc.vector.tensor_tensor(small[:, o + 16:o + 20], small[:, o + 12:o + 16],
                                                     small[:, o + 16:o + 20], ALU.add))
                        link(nc.vector.reciprocal(small[:, o + 20:o + 24], small[:, o + 16:o + 20]))
                        rec = small[:, o + 20:o + 24].unsqueeze(2).broadcast_to([P, 4, 256 - lo])
                        nc.vector.tensor_tensor(pr, pr, rec, ALU.mult).then_inc(p_norm, 1)
                    elif s[0] == "gla_decays":
                        c = s[1]
                        cc = slice(c * P, (c + 1) * P)
                        e = edec[:, c % 2, :]
                        if c == 0:
                            left(dve, GROUP[("turn_v", U_GG - 1, NTT - 1)])
                            dve.wait_ge(pv_full, 2 * NCH + 2)
                            dve.wait_ge(gates_ready, PAIRS * NTT)
                        if c >= 2:
                            dve.wait_ge(ga_full, c - 1)
                            dve.wait_ge(kd_turned, c - 1)
                        b3 = bg[:, :, cc]
                        ref = b3.rearrange("p q (i n) -> p q i n", i=NSUB)[:, :, :, SUB // 2 - 1:SUB // 2]
                        for p in range(PAIRS):
                            nc.vector.tensor_tensor(
                                e[:, 512 * p:512 * p + 512].rearrange("p (i n) -> p i n", i=NSUB),
                                ref[:, p].broadcast_to([P, NSUB, P]),
                                b3[:, p].unsqueeze(1).broadcast_to([P, NSUB, P]), ALU.subtract)
                        link(nc.vector.tensor_tensor(
                            e[:, 1024:1280].rearrange("p (q i n) -> p q i n", q=PAIRS, i=NSUB),
                            b3.rearrange("p q (i n) -> p q i n", i=NSUB),
                            ref.broadcast_to([P, PAIRS, NSUB, SUB]), ALU.subtract))
                        nc.vector.tensor_scalar(e[:, 0:1280], e[:, 0:1280], CLAMP, None, ALU.min)
                        nc.vector.tensor_tensor(
                            e[:, 1280:1536].rearrange("p (q n) -> p q n", q=PAIRS),
                            b3[:, :, P - 1:P].broadcast_to([P, PAIRS, P]), b3, ALU.subtract).then_inc(dec_ready, 1)
                        dve.wait_ge(dec_exp, c + 1)
                        if c > 1:
                            dve.wait_ge(s_ready, c - 1)
                        for p in range(PAIRS):
                            ek = e[:, 512 * p:512 * p + 512].rearrange("p (i n) -> p i n", i=NSUB)
                            nc.vector.tensor_tensor(ek, ek, kg[:, p, cc].unsqueeze(1).broadcast_to([P, NSUB, P]),
                                                    ALU.mult)
                        eq = e[:, 1024:1280].rearrange("p (q n) -> p q n", q=PAIRS)
                        nc.vector.tensor_tensor(eq, eq, qg[:, :, cc], ALU.mult)
                        ed = e[:, 1280:1536].rearrange("p (q n) -> p q n", q=PAIRS)
                        nc.vector.tensor_tensor(ed, ed, kg[:, :, cc], ALU.mult)
                        k_ = 48 + 2 * (c % 2)
                        link(nc.vector.tensor_copy(small[:, k_:k_ + 2].unsqueeze(2), qh[:, c % 2, :, P - 1:P]))
                        nc.vector.tensor_tensor(qh[:, c % 2, :, :], qh[:, c % 2, :, :], qg[:, :, cc],
                                                ALU.mult).then_inc(dec_mult, 1)
                    elif s[0] == "gla_scores":
                        c = s[1]
                        dve.wait_ge(ga_full, c + 1)
                        if c >= 2:
                            dve.wait_ge(go_full, c - 1)
                        for hd in range(GH):
                            o = 512 * (hd % 2) + hd // 2 * P
                            last = nc.vector.copy_predicated(asb[:, c % 2, hd, :], c_("causal").bitcast(u32),
                                                             pair_a[:, o:o + P])
                        last.then_inc(ga_masked, 1)
                    elif s[0] == "gla_state_sum":
                        c = s[1]
                        dve.wait_ge(ds_full, c + 1)
                        if c > 0:
                            dve.wait_ge(go_full, c + 1)
                        if c > 0:
                            dve.wait_ge(s_ready, c)
                        else:
                            left(dve, GROUP[("gate", PAIRS - 1, NTT - 1)])
                            link(nc.vector.memset(st[:], 0.0))
                        for hd in range(GH):
                            p, r = hd // 2, slice(64 * (hd % 2), 64 * (hd % 2) + 64)
                            add = pair_b[r, 512 + p * P:512 + (p + 1) * P]
                            k_ = 48 + 2 * (c % 2) + p
                            if c == 0:
                                last = nc.vector.tensor_copy(st[r, hd, :], add)
                            else:
                                last = nc.vector.scalar_tensor_tensor(st[r, hd, :], st[r, hd, :],
                                                                      small[r, k_:k_ + 1], add,
                                                                      ALU.mult, ALU.add)
                        last.then_inc(s_ready, 1)
                    elif s[0] == "gla_norm":
                        c = s[1]
                        w = P if c < NCH else NS
                        dve.wait_ge(gn_rstd, c + 1)
                        o = vo[:, c, :, :] if c < NCH else o_s[:]
                        nc.vector.scalar_tensor_tensor(o, o, p_("g_gla"),
                                                       grstd[:, 0:GH * w].rearrange("p (h n) -> p h n", h=GH),
                                                       ALU.mult, ALU.mult).then_inc(gn_done, 1)
                    elif s[0] == "gla_sample":
                        b3 = bg[:, :, SEQ:T]
                        b4 = b3.rearrange("p q (b t) -> p q b t", b=NB)
                        dve.wait_ge(kd_turned, NCH)
                        dve.wait_ge(ga_full, NCH)
                        link(nc.vector.memset(asam[:], 0.0))
                        nc.vector.tensor_scalar(esam[:, 0], b3, -1.0, CLAMP, ALU.mult, ALU.min)
                        nc.vector.tensor_tensor(esam[:, 1].rearrange("p q (b t) -> p q b t", b=NB),
                                                b4[:, :, :, NT - 1:NT].broadcast_to([P, PAIRS, NB, NT]), b4,
                                                ALU.subtract).then_inc(dec_ready, 1)
                        dve.wait_ge(dec_exp, NCH + 1)
                        for e in range(2):
                            nc.vector.tensor_tensor(esam[:, e], esam[:, e], kg[:, :, SEQ:T], ALU.mult)
                        dec = qh[:, 0, :, 0:NS].rearrange("p q (b t) -> p b q t", b=NB)[:, :, :, NT - 1:NT]
                        keep = small[:, 0:16].rearrange("p (b q) -> p b q", b=NB)
                        link(nc.vector.tensor_copy(keep.unsqueeze(3), dec))
                        nc.vector.tensor_tensor(qh[:, 0, :, 0:NS], qh[:, 0, :, 0:NS], qg[:, :, SEQ:T],
                                                ALU.mult).then_inc(dec_mult, 1)
                        dve.wait_ge(ga_full, NCH + 1)
                        for hd in range(GH):
                            o = 512 * (hd % 2) + hd // 2 * NS
                            last = nc.vector.copy_predicated(asam[:, hd, :], c_("causal_s", NS).bitcast(u32),
                                                             pair_a[0:NS, o:o + NS])
                        last.then_inc(ga_masked, 1)
                        dve.wait_ge(kd_copied, NCH + 1)
                        for b in range(NB):
                            last = nc.vector.tensor_scalar(
                                kdm[:, b, :], kdn[0:NS, 0, :, :].rearrange("p q n -> p (q n)"),
                                c_("bmask", NS)[:, b:b + 1], None, ALU.mult)
                        last.then_inc(kd_copied, 1)
                        dve.wait_ge(ds_full, NCH + 1)
                        dve.wait_ge(go_full, NCH + 1)
                        link(nc.vector.tensor_tensor(s0[:], s0[:], keep.unsqueeze(3).broadcast_to([P, NB, PAIRS, P]),
                                                     ALU.mult))
                        for half, src in ((0, pair_a), (1, pair_b)):
                            part = s0[:, 4 * half:4 * half + 4, :, :]
                            last = nc.vector.tensor_tensor(part, part,
                                                           src[:].rearrange("p (b q v) -> p b q v", b=4, q=PAIRS),
                                                           ALU.add)
                        last.then_inc(s_ready, 1)
                    elif s[0] == "split_out":
                        tt = s[1]
                        nj = 3 if tt < NTT - 1 else 2
                        c0 = COLS[tt][0]
                        for k in range(KC):
                            dve.wait_ge(o_high, KC * tt + k + 1)
                            if k < GH:
                                if tt == 0:
                                    dve.wait_ge(sg_used, NTT * k + NTT)
                                hi = h_hi[:, k, c0:c0 + nj * P].rearrange("p (j n) -> p j n", j=nj)
                                lo = h_lo[:, k, c0:c0 + nj * P].rearrange("p (j n) -> p j n", j=nj)
                                last = nc.vector.tensor_tensor(lo, vo[:, 3 * tt:3 * tt + nj, k, :],
                                                               hi.bitcast(f32), ALU.subtract)
                                if tt == NTT - 1:
                                    last = nc.vector.tensor_tensor(h_lo[:, k, SEQ:T], o_s[:, k, :],
                                                                   h_hi[:, k, SEQ:T].bitcast(f32), ALU.subtract)
                            else:
                                last = nc.vector.tensor_tensor(h_lo[:, k, cols(tt)], qs[:, k - GH, cols(tt)],
                                                               h_hi[:, k, cols(tt)].bitcast(f32), ALU.subtract)
                            last.then_inc(o_ready, 1)

                with dve.Fori(0, FPAIRS) as i:
                    for f in range(2):
                        for tt in range(NTT + 1):
                            if tt < NTT:
                                w = width(tt)
                                j = NTT * (2 * f + 1) + tt
                                g = G_FF + j
                                n_done = NTT * f + tt
                                gate = g - NTT
                                dve.wait_ge(acc_free[gate % ACCS], i * (FF_GROUPS // ACCS) + (gate // ACCS + 1))
                                dve.wait_ge(acc_full, i * FF_GROUPS + (g + 1))
                                dve.wait_ge(hid_ready, i * (2 * NTT) + max(n_done - 1, 0))
                                nc.vector.tensor_tensor(tmp_a[:, n_done % 2, 0:w], silu_g[:, tt, 0:w],
                                                        bank(g)[:, 0:w], ALU.mult).then_inc(acc_free[g % ACCS], 1)
                            if tt > 0:
                                m = NTT * f + tt - 1
                                w = width(tt - 1)
                                dve.wait_ge(hid_high, i * (2 * NTT) + (m + 1))
                                nc.vector.tensor_tensor(hid_lo[:, f, cols(tt - 1)], tmp_a[:, m % 2, 0:w],
                                                        hid_hi[:, f, cols(tt - 1)].bitcast(f32),
                                                        ALU.subtract).then_inc(hid_ready, 1)
                    for j in range(2):
                        for tt in range(NTT):
                            for d in range(4):
                                g = G_FF + 4 * NTT + 4 * (NTT * j + tt) + d
                                dve.wait_ge(acc_full, i * FF_GROUPS + (g + 1))
                                xs = x[:, 4 * j + d, cols(tt)]
                                nc.vector.tensor_tensor(xs, xs, bank(g)[:, 0:width(tt)],
                                                        ALU.add).then_inc(acc_free[g % ACCS], 1)

        nc.sync.sem_clear(layer_sems)
        nc.all_engine_barrier()

    with nc.Block() as block:
        @block.scalar
        def _(act):
            for tt in range(NTT):
                w = width(tt)
                for k in range(KC):
                    if k == 0:
                        if tt >= 2:
                            act.wait_ge(fin["full"], tt - 1)
                        dst = ssum[:, tt % 2, 0:w]
                    else:
                        taken = (KC - 1) * tt + max(k - 2, 0)
                        if taken > 0:
                            act.wait_ge(fin["added"], taken)
                        dst = sqt[:, k % 2, 0:w]
                    nc.scalar.activation(dst, x[:, k, cols(tt)], ACT.Square).then_inc(fin["square"], 1)
            for tt in range(NTT):
                w = width(tt)
                act.wait_ge(fin["full"], tt + 1)
                if tt > 0:
                    act.wait_ge(fin["out"], KC * tt)
                nc.scalar.activation(rstd[:, 0:w], acc[tt][:, 0:w], ACT.Ln, bias=c_("eps"),
                                     scale=1.0 / D_MODEL).then_inc(fin["ln"], 1)
                act.wait_ge(fin["ln"], tt + 1)
                nc.scalar.activation(rstd[:, 0:w], rstd[:, 0:w], ACT.Exp, scale=-0.5).then_inc(fin["rstd"], 1)

        @block.tensor
        def _(pe):
            for tt in range(NTT):
                w = width(tt)
                pe.wait_ge(fin["added"], (KC - 1) * (tt + 1))
                nc.tensor.matmul(acc[tt][:, 0:w], c_("ones"), ssum[:, tt % 2, 0:w], start=True,
                                 stop=True).then_inc(fin["full"], 1)

        @block.vector
        def _(dve):
            for tt in range(NTT):
                w = width(tt)
                for k in range(1, KC):
                    dve.wait_ge(fin["square"], KC * tt + k + 1)
                    if k > 1:
                        dve.wait_ge(fin["added"], (KC - 1) * tt + k - 1)
                    nc.vector.tensor_tensor(ssum[:, tt % 2, 0:w], ssum[:, tt % 2, 0:w], sqt[:, k % 2, 0:w],
                                            ALU.add).then_inc(fin["added"], 1)
            for tt in range(NTT):
                w = width(tt)
                dve.wait_ge(fin["rstd"], tt + 1)
                for k in range(KC):
                    nc.vector.scalar_tensor_tensor(x[:, k, cols(tt)], x[:, k, cols(tt)], gfin[:, k:k + 1],
                                                   rstd[:, 0:w], ALU.mult, ALU.mult).then_inc(fin["out"], 1)

        @block.sync
        def _(sp):
            for tt in range(NTT):
                for half in range(2):
                    sp.wait_ge(fin["out"], KC * tt + KC // 2 * (half + 1))
                    kk = slice(KC // 2 * half, KC // 2 * (half + 1))
                    sp.dma_start(y_t[:, kk, cols(tt)], x[:, kk, cols(tt)]).then_inc(fin["stored"], 16)
            sp.wait_ge(fin["stored"], 16 * 2 * NTT)


def shape_constants(np):
    CO, n = offsets(CONSTS)
    const = np.zeros((P, n), np.float32)
    i = np.arange(P)
    const[:, slice(*CO["ident"])] = np.eye(P)
    const[:, slice(*CO["ones"])] = 1.0
    key = np.arange(256)[None] - P
    ok = (key <= i[:, None]) & (i[:, None] - key < WCACHE)
    const[:, slice(*CO["band"])] = np.where(ok, 0.0, NEG)
    const[:, slice(*CO["eps"])] = EPS
    j = np.arange(NS)
    const[:, slice(*CO["reset"])] = (j % NT != 0)[None]
    const[0:NS, slice(*CO["bmask"])] = j[:, None] // NT == np.arange(NB)[None]
    const[:, slice(*CO["causal"])] = i[:, None] <= i[None]
    const[0:NS, slice(*CO["causal_s"])] = (j[:, None] <= j[None]) & (j[:, None] // NT == j[None] // NT)
    row = np.arange(P)
    rb, rt = row % NS // NT, row % NT
    dec = np.full((P, T), NEG, np.float32)
    kb, kj = np.arange(SEQ) // WCACHE, np.arange(SEQ) % WCACHE
    dec[:, 0:SEQ][(kb[None] == rb[:, None]) & (kj[None] > rt[:, None])] = 0.0
    dec[:, SEQ:][(j[None] // NT == rb[:, None]) & (j[None] % NT <= rt[:, None])] = 0.0
    pos = np.concatenate([np.arange(SEQ), SEQ + j % NT]).astype(np.float32)
    half = 32
    inv = np.float32(10000.0) ** (-np.arange(half, dtype=np.float32) / np.float32(half))
    ang = (pos[None] * inv[i % half][:, None]).astype(np.float32).astype(np.float64)
    sign = np.where(i % 64 < half, -1.0, 1.0)[:, None]
    tables = np.stack([np.cos(ang), sign * np.sin(ang)], 1).astype(np.float32)
    return const, tables, dec


def weight_units(np, w_in, w_o, w_gate, w_up, w_down):
    L = w_in.shape[0]

    def tiles(w):
        n = w.shape[2] // P
        return w.reshape(L, KC, P, n, P).transpose(0, 3, 2, 1, 4).reshape(L, n, P, UNIT)

    gq, gk, gv, ga, gg, sq, sk, sv = np.split(w_in, [256, 512, 1024, 1040, 1552, 2064, 2192], axis=2)
    ga = np.concatenate([ga, np.zeros((L, D_MODEL, P - 16), w_in.dtype)], axis=2)
    sq = sq.reshape(L, D_MODEL, 2, 4, 64).transpose(0, 1, 3, 2, 4).reshape(L, D_MODEL, 512)
    wo_swa = w_o[:, 512:].reshape(L, 2, 4, 64, D_MODEL).transpose(0, 2, 1, 3, 4).reshape(L, 512, D_MODEL)
    wo = np.concatenate([w_o[:, :512], wo_swa], axis=1)
    gate, up = (tiles(w).reshape(L, FPAIRS, 2, 1, P, UNIT) for w in (w_gate, w_up))
    gu = np.concatenate([gate, up], axis=3).reshape(L, FPAIRS, 4, P, UNIT)
    down = w_down.reshape(L, FPAIRS, 2, P, 2, 4, P).transpose(0, 1, 4, 3, 2, 5, 6).reshape(L, FPAIRS, 2, P, UNIT)
    ff = np.concatenate([gu, down], axis=2).reshape(L, FPAIRS * 6, P, UNIT)
    return np.concatenate([tiles(w) for w in (sk, sv, sq, gk, gq, ga, gv, gg, wo)] + [ff], axis=1)


def layer_params(np, norm_attn, norm_ffn, gla_norm, b_gk2, attn_sinks):
    L = norm_attn.shape[0]
    cols = lambda a: a.reshape(L, -1, P).transpose(0, 2, 1)
    every = lambda a: np.broadcast_to(a[:, None, :], (L, P, a.shape[1]))
    rows = lambda a: np.repeat(a.reshape(L, 2, 4), NS, axis=2).transpose(0, 2, 1)
    return np.concatenate([cols(norm_attn), cols(norm_ffn), cols(gla_norm), cols(b_gk2),
                           every(attn_sinks), rows(attn_sinks)], axis=2)


def kernel(**inputs):
    import numpy as np
    import concourse.bacc as _bacc
    from concourse.bass_utils import run_bass_kernel_spmd as _run

    a = {k: np.asarray(v) for k, v in inputs.items()}
    L = DEPTH
    const, tables, dec = shape_constants(np)
    x_all = np.concatenate([a["x_prompt"].reshape(SEQ, D_MODEL), a["x_sample"].reshape(NS, D_MODEL)])
    arrays = {
        "x_t": x_all.reshape(T, KC, P).transpose(2, 1, 0),
        "units": weight_units(np, a["w_in"], a["w_o"], a["w_gate"], a["w_up"], a["w_down"]),
        "consts": const, "tables": tables, "dec_mask": dec,
        "params": layer_params(np, a["norm_attn"], a["norm_ffn"], a["gla_norm"], a["b_gk2"],
                               a["attn_sinks"]),
        "w_gk2": a["w_gk2"],
        "state_in": a["state_gla"].reshape(L, NB, GH * 64, P),
        "kcache_t": a["cache_swa_k"].reshape(L, NB, WCACHE, P).transpose(0, 3, 1, 2),
        "kcache": a["cache_swa_k"].reshape(L, NB, WCACHE, P),
        "vcache": a["cache_swa_v"].reshape(L, NB, WCACHE, P),
        "norm_final": a["norm_final"].reshape(KC, P).T,
    }
    arrays = {k: np.ascontiguousarray(v) for k, v in arrays.items()}
    outs = {
        "y_t": (P, KC, T), "state_p": (L, 1, GH * 64, P), "kc_p": (L, 1, WCACHE, P),
        "vc_p": (L, 1, WCACHE, P), "state_s": (L, NB, GH * 64, P), "kc_s": (L, NB, WCACHE, P),
        "vc_s": (L, NB, WCACHE, P),
    }
    nc = _bacc.Bacc("TRN2", target_bir_lowering=False, num_devices=1, dynamic_dma_scratch_size=256)
    args = [nc.dram_tensor(k, v.shape, mybir.dt.from_np(v.dtype), kind="ExternalInput").ap()
            for k, v in arrays.items()]
    args += [nc.dram_tensor(k, s, mybir.dt.float32, kind="ExternalOutput").ap() for k, s in outs.items()]
    trunk(nc, *args)
    r = _run(nc, [arrays], core_ids=[0]).results[0]
    y = np.asarray(r["y_t"]).transpose(2, 1, 0).reshape(T, D_MODEL)
    cache = lambda name, n: np.asarray(r[name]).reshape(L, n, WCACHE, 2, 64)
    return (y[:SEQ].reshape(1, SEQ, D_MODEL), y[SEQ:].reshape(NB, NT, D_MODEL),
            np.asarray(r["state_p"]).reshape(L, 1, GH, 64, P), cache("kc_p", 1), cache("vc_p", 1),
            np.asarray(r["state_s"]).reshape(L, NB, GH, 64, P), cache("kc_s", NB), cache("vc_s", NB))
```

```python
import concourse.bass as bass
from concourse import mybir

D_MODEL = 1024
DEPTH = 2
SEQ = 1024
NB, NT = 8, 4
NS = NB * NT
T = SEQ + NS
P = 128
KC = D_MODEL // P
D_FF = 2816
FT = D_FF // P
FPAIRS = FT // 2
COLS = ((0, 384), (384, 768), (768, T))
NTT = len(COLS)
TW = 384
RANK = 16
NCH = SEQ // P
GH = 4
PAIRS = GH // 2
SUB = 32
NSUB = P // SUB
WCACHE = 128
EPS = 1e-6
GATE_NORM = 16.0
CLAMP = 80.0 * GATE_NORM
UNIT = KC * P
RING = 2
SQR = 3
POOL_LOWS = (1, 4, 7)
DVE_LOWS = tuple(k for k in range(KC) if k not in POOL_LOWS)
ACCS = 3
NEG = -1.0e30

U_SK, U_SV, U_SQ, U_GK, U_GQ, U_GA, U_GV, U_GG, U_WO = 0, 1, 2, 6, 8, 10, 11, 15, 19
U_FF = 27
UNITS = U_FF + 6 * FPAIRS
FF_UNITS = 6
FF_GROUPS = 4 * NTT + KC * NTT

CONSTS = {"ident": 128, "ones": 128, "band": 256, "reset": 32, "bmask": NB,
          "causal": 128, "causal_s": 32, "eps": 1}
PARAMS = {"g_attn": KC, "g_ffn": KC, "g_gla": 1, "b_gate": PAIRS, "sink": 8, "sink_rows": 2}


LN_EXP = "natural_log_exp_and_others"


def offsets(table):
    at, out = 0, {}
    for name, n in table.items():
        out[name] = (at, at + n)
        at += n
    return out, at


def schedule():
    steps = []

    def squares(n, tt, ks=range(KC)):
        steps.extend(("square", n, tt, k) for k in ks)

    def normed(n, tt, half=None):
        return [("normed", n, tt, h) for h in range(2) if half is None or h == half]

    def project(u, tt):
        return [("z", u, tt), ("take", u, tt)]

    squares(0, 0)
    steps += [("stat", 0, 0)]
    squares(0, 1)
    steps += [("rstd", 0, 0), ("stat", 0, 1), ("rstd", 0, 1)] + normed(0, 0)
    steps += [("z", U_SK, 0)] + normed(0, 1) + [("z", U_SK, 1)]
    squares(0, 2)
    steps += [("stat", 0, 2), ("rstd", 0, 2), ("take", U_SK, 0)]
    steps += normed(0, 2) + [("z", U_SK, 2), ("take", U_SK, 1), ("park",), ("take", U_SK, 2)]
    held = []
    for u in range(U_SV, U_GK):
        for tt in range(NTT):
            steps += project(u, tt) + held
            held = [("turn_v", u, tt)] if u == U_SV else []
    rest = []
    for u in range(U_GK, U_GG):
        for tt in range(NTT):
            rest.append(project(u, tt) + held)
            held = [("turn_v", u, tt)] if u >= U_GV else []
            if u == U_GA:
                if tt == 1:
                    rest[-1] += [("gate", 0, 0)]
                if tt == 2:
                    rest[-1] = [("z", u, tt), ("gate", 1, 0), ("take", u, tt)]
            if u == U_GV:
                gates = [("gate", 0, 1), ("gate", 1, 1), ("gate", 0, 2)]
                rest[-1] += [gates[tt]]
            if u == U_GV + 1 and tt == 0:
                rest[-1] += [("gate", 1, 2)]
    rest.append(held)
    steps.append(("turn_k",))
    for g in range(2):
        steps += [("dec_scores", g)] + rest[2 * g] + [("dec_norm", g), ("dec_turn", g)] + rest[2 * g + 1]
        steps += [("dec_values", g)]
    items = 2 * NCH
    first = done = 4
    for n in range(items + 1):
        if n < items:
            steps.append(("scores", n))
        if n > 0:
            steps.append(("norm_p", n - 1))
        if n > 1:
            steps.append(("values", n - 2))
        upto = first + (len(rest) - first) * (n + 1) // (items + 1)
        half = done + (upto - done + 1) // 2
        for r in rest[done:half]:
            steps += r
        if n > 0:
            steps += [("turn_p", n - 1)]
        for r in rest[half:upto]:
            steps += r
        done = upto
        if n < items:
            steps.append(("exp_p", n))
    steps.append(("values", items - 1))
    gate = [(u, tt) for u in range(U_GG, U_WO) for tt in range(NTT)]
    def exponents(c):
        return [("gla_exponents", c) if c < NCH else ("sample_exponents",)]

    def exps(c):
        return [("gla_exps", c) if c < NCH else ("sample_exps",)]

    def decays(c):
        return [("gla_decays", c) if c < NCH else ("sample_decays",)]

    steps += exponents(0) + exps(0) + project(*gate[0]) + decays(0) + exponents(1) + exps(1)
    for c in range(NCH):
        steps += [("gla_scores", c), ("gla_turn", c), ("gla_mask", c)] + decays(c + 1)
        if c > 1:
            steps.append(("gla_scale", c - 2))
        if c + 2 <= NCH:
            steps += exponents(c + 2)
        if c > 0:
            steps.append(("gla_square", c - 1))
        steps.append(("z",) + gate[c + 1])
        if c > 0:
            steps.append(("gla_stat", c - 1))
        steps += [("take",) + gate[c + 1], ("gla_state", c), ("gla_out", c), ("gla_state_sum", c)]
        if c + 2 <= NCH:
            steps += exps(c + 2)
        if c > 0:
            steps.append(("gla_rstd", c - 1))
    steps += [("sample_scores",), ("gla_square", NCH - 1), ("gla_scale", NCH - 2)] + project(*gate[9])
    steps += [("sample_out",), ("gla_stat", NCH - 1), ("gla_square", NCH), ("gla_stat", NCH),
              ("gla_rstd", NCH - 1), ("gla_scale", NCH - 1), ("gla_rstd", NCH), ("gla_scale", NCH)]
    mixed = [*range(GH, KC), *range(GH)]
    steps += [("z",) + gate[10]] + [("split", k, 0) for k in mixed[:GH]]
    steps += [("silu", hd) for hd in range(GH - 1)] + [("take",) + gate[10], ("z",) + gate[11]]
    steps += [("gate_out", hd) for hd in range(GH - 1)]
    steps += [("take",) + gate[11], ("silu", GH - 1)] + [("split", k, 0) for k in range(GH - 1)]
    steps += [("gate_out", GH - 1), ("split", GH - 1, 0), ("unpark",)]
    steps += [("split", k, tt) for tt in range(1, NTT) for k in mixed]
    for k in range(KC - 1):
        for tt in range(NTT):
            steps += project(U_WO + k, tt)
            if k > 0 or tt > 0:
                squares(1, (tt - 1) % NTT, [k if tt > 0 else k - 1])
    k, u = KC - 1, U_FF - 1
    steps += [("z", u, 0)]
    squares(1, NTT - 1, [k - 1])
    steps += [("take", u, 0)]
    squares(1, 0, [k])
    steps += [("z", u, 1), ("stat", 1, 0), ("rstd", 1, 0), ("take", u, 1)]
    squares(1, 1, [k])
    steps += [("z", u, 2)] + normed(1, 0, 0) + [("stat", 1, 1), ("take", u, 2)]
    squares(1, 2, [k])
    steps += [("sample_states",), ("stat", 1, 2), ("rstd", 1, 1)] + normed(1, 0, 1) + [("rstd", 1, 2)]
    steps += normed(1, 1) + normed(1, 2) + [("sample_sum",)]
    return steps


GROUP_STEPS = ("z", "stat", "turn_v", "turn_k", "gate", "gla_stat")


def group_numbers(steps):
    table, n = {}, 0
    for s in steps:
        if s[0] in GROUP_STEPS:
            table[s] = n
            n += 1
    return table, n


def count_before(steps, kind, step):
    n = 0
    for s in steps:
        if s == step:
            return n
        n += s[0] == kind
    raise ValueError(step)


def trunk(nc, x_t, units, consts, tables, dec_mask, params, w_gk2, state_in, kcache_t,
          kcache, vcache, norm_final, park, y_t, state_p, kc_p, vc_p, state_s, kc_s, vc_s):
    f32, f32r, u32 = mybir.dt.float32, mybir.dt.float32r, mybir.dt.uint32
    ALU = mybir.AluOpType
    ACT = mybir.ActivationFunctionType
    AX = mybir.AxisListType
    STEPS = schedule()
    GROUP, G_FF = group_numbers(STEPS)
    SQUARE = {s: n for n, s in enumerate(s for s in STEPS if s[0] == "square")}
    ADDED = {s: n for n, s in enumerate(s for s in STEPS if s[0] == "square" and s[3] > 0)}
    SPLIT = {s: n for n, s in enumerate(s for s in STEPS if s[0] == "split")}
    CO, NCONST = offsets(CONSTS)
    PO, NPARAM = offsets(PARAMS)

    base = (nc.sbuf_base + 31) // 32 * 32
    top = [base]

    def region(nbytes):
        at = top[0]
        top[0] += (nbytes + 31) // 32 * 32
        return at

    def at(name, offset, shape, dt=f32):
        return nc.alloc_sbuf_tensor_at(name, shape, dt, offset=offset)

    x = at("x", region(KC * T * 4), [P, KC, T])
    h_hi = at("h_hi", region(KC * T * 4), [P, KC, T], f32r)
    h_lo = at("h_lo", region(KC * T * 4), [P, KC, T], f32r)
    w_raw = at("w_raw", region(RING * UNIT * 4), [P, RING, UNIT])
    w_hi = at("w_hi", region(RING * UNIT * 4), [P, RING, UNIT], f32r)
    w_lo = at("w_lo", region(RING * UNIT * 4), [P, RING, UNIT], f32r)
    const = at("const", region(NCONST * 4), [P, NCONST])
    par = at("par", region((NPARAM + KC + 10) * 4), [P, NPARAM + KC + 10])
    gfin = par[:, NPARAM:NPARAM + KC]
    nsink = par[:, NPARAM + KC:NPARAM + KC + 10]
    r_qs, r_ks, r_sv = region(4 * T * 4), region(T * 4), region(9 * P * 4)
    qs = at("qs", r_qs, [P, 4, T])
    ks = at("ks", r_ks, [P, T])
    sv = at("sv", r_sv, [P, 9, P])
    s0 = at("s0", r_ks, [P, NB, PAIRS, P])
    r_qg, r_kg, r_bg, r_vo = (region(PAIRS * T * 4), region(PAIRS * T * 4),
                              region(PAIRS * T * 4), region(9 * GH * P * 4))
    qg = at("qg", r_qg, [P, PAIRS, T])
    kg = at("kg", r_kg, [P, PAIRS, T])
    bg = at("bg", r_bg, [P, PAIRS, T])
    vo = at("vo", r_vo, [P, 9, GH, P])
    rope = at("rope", r_bg, [P, 2, T])
    dmask = at("dmask", r_vo, [P, T])
    kct = at("kct", r_vo + T * 4, [P, NB, WCACHE])
    vct = at("vct", r_vo + T * 4 + NB * WCACHE * 4, [P, NB, P])
    r_spare = r_vo + (T + 2 * NB * WCACHE) * 4
    gk2 = at("gk2", r_spare, [2 * RANK, PAIRS * P])
    kno = at("kno", r_spare + 1024, [P, 2, P])
    dnew_t = at("dnew_t", r_spare + 2048, [NS, P])
    dq = at("dq", r_spare + 2560, [P, 4 * NS])
    r_big = region(3 * 4 * 256 * 4)
    prob = at("prob", r_big, [P, 2, 4, 256])
    prob_t = at("prob_t", r_big + 2 * 4 * 256 * 4, [P, 2, 4, P])
    dprob = at("dprob", r_big, [P, T])
    dprob_t = at("dprob_t", r_big + 2 * 4 * 256 * 4, [P, NB, P])
    edec = at("edec", r_big, [P, 2, 6 * 256])
    kdm = at("kdm", r_big + 4096, [NS, NB, PAIRS * P])
    esam = at("esam", r_big, [P, 2, 2, NS])
    r_t = region(4 * TW * 4)
    tmp_a = at("tmp_a", r_t, [P, 2, TW])
    tmp_n = at("tmp_n", r_t, [P, 4, TW])
    tmp_b = at("tmp_b", r_t + 2 * TW * 4, [P, 2, TW])
    r_rstd = region(TW * 4)
    rstds = at("rstds", r_kg + TW * 4, [P, NTT, TW])
    sqt = at("sqt", region(2 * TW * 4), [P, 2, TW])
    sqr = at("sqr", r_rstd, [P, SQR, TW])
    r_sum = region(2 * TW * 4)
    ssum = at("ssum", r_sum, [P, 2, TW])
    gat = at("gat", r_sum, [2 * RANK, 2, TW])
    sums = [ssum[:, 0, :], ssum[:, 1, :], at("ssum_c", r_kg, [P, TW])[:]]
    gsq = at("gsq", r_rstd, [P, GH * P])
    grstd = at("grstd", r_rstd + GH * P * 4, [P, GH * P])
    o_s = at("o_s", r_qg + T * 4, [P, GH, NS])
    small = at("small", region(52 * 4), [P, 52])
    qh = at("qh", r_t + 2 * TW * 4, [P, 2, PAIRS, P])
    kdn = at("kdn", r_t, [P, 2, PAIRS, P])
    qpad = [at(f"qpad{p}", r_t + 2 * TW * 4 * p + 2048, [P, NSUB, 2, SUB]) for p in range(PAIRS)]
    asb = at("asb", region(2 * GH * P * 4), [P, 2, GH, P])
    asam = at("asam", r_big + 2048, [NS, GH, NS])
    qz = at("qz", r_big + 1024, [P, PAIRS, 2, NS])
    st = at("st", r_sum, [P, GH, P])
    hid_hi = at("hid_hi", r_qs, [P, 2, T], f32r)
    hid_lo = at("hid_lo", r_qs + 2 * T * 4, [P, 2, T], f32r)
    silu_g = at("silu_g", r_qg, [P, NTT, TW])
    assert top[0] <= nc.sbuf_usable_end, (top[0], nc.sbuf_usable_end)

    acc = [nc.alloc_psum_tensor(f"acc{b}", [P, 512], f32) for b in range(ACCS)]
    pair_a = nc.alloc_psum_tensor("pair_a", [P, 1024], f32)
    pair_b = nc.alloc_psum_tensor("pair_b", [P, 1024], f32)
    single = nc.alloc_psum_tensor("single", [P, 512], f32)

    def sem(name):
        return nc.alloc_semaphore(name)

    set_up = sem("set_up")
    x_in = [sem(f"x_in{tt}") for tt in range(NTT)]
    fin_in = sem("fin_in")
    zeroed = sem("zeroed")
    fin = {n: sem(f"fin_{n}") for n in ("square", "full", "ln", "rstd", "out", "stored")}
    acc_full = sem("acc_full")
    acc_free = [sem(f"acc_free{b}") for b in range(ACCS)]
    w_loaded = [sem(f"w_loaded{s}") for s in range(RING)]
    w_high = sem("w_high")
    ga_low = sem("ga_low")
    w_ready = sem("w_ready")
    par_loaded = sem("par_loaded")
    rope_loaded = sem("rope_loaded")
    gk2_loaded = sem("gk2_loaded")
    loaded = sem("loaded")
    s0_loaded = sem("s0_loaded")
    state_stored = sem("state_stored")
    parked = sem("parked")
    unparked = sem("unparked")
    silu_made = sem("silu_made")
    out_sem = sem("out_sem")
    dve_chain = sem("dve_chain")
    act_chain = sem("act_chain")
    squares = sem("squares")
    sq_added = sem("sq_added")
    rstd_ready = sem("rstd_ready")
    hf_made = sem("hf_made")
    hi_made = sem("hi_made")
    h_ready = sem("h_ready")
    h_pool = sem("h_pool")
    roped = sem("roped")
    gate_log = sem("gate_log")
    gates_ready = sem("gates_ready")
    dq_packed = sem("dq_packed")
    sc_full = sem("sc_full")
    sc_read = sem("sc_read")
    max_ready = sem("max_ready")
    p_exp = sem("p_exp")
    p_norm = sem("p_norm")
    pt_full = sem("pt_full")
    pt_copied = sem("pt_copied")
    pv_full = sem("pv_full")
    pv_copied = sem("pv_copied")
    dec_ready = sem("dec_ready")
    dec_exp = sem("dec_exp")
    dec_mult = sem("dec_mult")
    ga_full = sem("ga_full")
    ga_masked = sem("ga_masked")
    kd_turned = sem("kd_turned")
    kd_copied = sem("kd_copied")
    ds_full = sem("ds_full")
    s_ready = sem("s_ready")
    go_full = sem("go_full")
    go_copied = sem("go_copied")
    gn_square = sem("gn_square")
    gn_rstd = sem("gn_rstd")
    gn_done = sem("gn_done")
    sg_used = sem("sg_used")
    o_high = sem("o_high")
    o_ready = sem("o_ready")
    hid_high = sem("hid_high")
    hid_ready = sem("hid_ready")
    layer_sems = range(acc_full.num, hid_ready.num + 1)

    def c_(name, rows=P):
        a, b = CO[name]
        return const[0:rows, a:b]

    def p_(name, i=None, n=1):
        a, b = PO[name]
        return par[:, a:b] if i is None else par[:, a + i:a + i + n]

    def bank(g):
        return acc[g % ACCS]

    def left(eng, g):
        eng.wait_ge(acc_free[g % ACCS], g // ACCS + 1)

    def split_in(eng, m, k):
        if k in POOL_LOWS:
            eng.wait_ge(h_pool, len(POOL_LOWS) * m + POOL_LOWS.index(k) + 1)
        else:
            eng.wait_ge(h_ready, len(DVE_LOWS) * m + DVE_LOWS.index(k) + 1)

    def width(tt):
        return COLS[tt][1] - COLS[tt][0]

    def cols(tt):
        return slice(*COLS[tt])

    with nc.Block() as block:
        @block.sync
        def _(sp):
            sp.dma_start(x[:, :, cols(0)], x_t[:, :, cols(0)]).then_inc(x_in[0], 16)
            sp.dma_start(const[:], consts).then_inc(set_up, 16)
            sp.dma_start(x[:, :, cols(1)], x_t[:, :, cols(1)]).then_inc(x_in[1], 16)
            sp.dma_start(x[:, :, cols(2)], x_t[:, :, cols(2)]).then_inc(x_in[2], 16)
            sp.dma_start(gfin, norm_final).then_inc(fin_in, 16)

        @block.vector
        def _(dve):
            nc.vector.memset(asb[:], 0.0).then_inc(zeroed, 1)
            dve.wait_ge(zeroed, 1)

    with nc.Fori(0, DEPTH) as layer:
        with nc.Block() as block:

            @block.sync
            def _(sp):
                sp.dma_start(par[:, 0:NPARAM], params[layer]).then_inc(par_loaded, 16)
                for u in range(U_FF):
                    if u == RING:
                        for half in range(2):
                            sp.dma_start(gk2[RANK * half:RANK * (half + 1), :],
                                         w_gk2[layer]).then_inc(gk2_loaded, 16)
                        sp.dma_start(rope[:], tables).then_inc(rope_loaded, 16)
                    if u >= RING:
                        sp.wait_ge(w_ready, u - RING + 1)
                    sp.dma_start(w_raw[:, u % RING, :], units[layer, u]).then_inc(w_loaded[u % RING], 16)
                for j in range(FF_UNITS):
                    u = U_FF + j
                    sp.wait_ge(w_ready, u - RING + 1)
                    sp.dma_start(w_raw[:, u % RING, :], units[layer, u]).then_inc(w_loaded[u % RING], 16)
                    if j == RING:
                        sp.wait_ge(s_ready, NCH + 1)
                        sp.dma_start(state_s[layer].rearrange("b (q r) v -> r b q v", r=P), s0[:])\
                          .then_inc(out_sem, 16)
                with sp.Fori(1, FPAIRS) as i:
                    for j in range(FF_UNITS):
                        u = U_FF + j
                        sp.wait_ge(w_ready, i * FF_UNITS + (u - RING + 1))
                        sp.dma_start(w_raw[:, u % RING, :],
                                     units[layer, i * FF_UNITS + u]).then_inc(w_loaded[u % RING], 16)

            @block.gpsimd
            def _(pool):
                def split(u, loads, high, freed):
                    s = u % RING
                    if freed is not None:
                        pool.wait_ge(acc_full, freed)
                    pool.wait_ge(w_loaded[s], loads)
                    nc.gpsimd.tensor_tensor(w_hi[:, s, 0:SUB], w_raw[:, s, 0:SUB], c_("ones")[:, 0:SUB],
                                            ALU.mult)
                    nc.gpsimd.tensor_scalar(w_hi[:, s, SUB:], w_raw[:, s, SUB:], 1.0, 0.0,
                                            ALU.mult, ALU.add).then_inc(w_high, 1)
                    pool.wait_ge(w_high, high)
                    low = nc.gpsimd.tensor_tensor(w_lo[:, s, :], w_raw[:, s, :], w_hi[:, s, :].bitcast(f32),
                                                  ALU.subtract)
                    if u != U_GA:
                        low.then_inc(w_ready, 1)
                    else:
                        low.then_inc(ga_low, 1)
                        pool.wait_ge(ga_low, 1)
                        nc.gpsimd.tensor_scalar(
                            w_lo[:, s, :].rearrange("p (k n) -> p k n", k=KC)[:, :, 0:RANK],
                            w_raw[:, s, :].rearrange("p (k n) -> p k n", k=KC)[:, :, 0:RANK], 1.0, 0.0,
                            ALU.mult, ALU.add).then_inc(w_ready, 1)

                def lows(n, tt):
                    m = NTT * n + tt
                    for k in POOL_LOWS:
                        pool.wait_ge(hi_made, KC * m + k + 1)
                        nc.gpsimd.tensor_tensor(h_lo[:, k, cols(tt)], tmp_n[:, k % 4, 0:width(tt)],
                                                h_hi[:, k, cols(tt)].bitcast(f32),
                                                ALU.subtract).then_inc(h_pool, 1)

                pool.wait_ge(set_up, 16)
                for u in range(U_FF):
                    split(u, 16 * (u // RING + 1), u + 1,
                          GROUP[("z", u - RING, NTT - 1)] + 1 if u >= RING else None)
                    if u == 0:
                        lows(0, 0)
                    elif u == 1:
                        lows(0, 1)
                        lows(0, 2)
                ends = [NTT * (j + 1) for j in range(4)] + [4 * NTT + 4 * NTT * (j + 1) for j in range(2)]
                before = [ends[4] - FF_GROUPS, ends[5] - FF_GROUPS] + ends[0:4]
                for j in range(FF_UNITS):
                    u = U_FF + j
                    freed = GROUP[("z", u - RING, NTT - 1)] + 1 if j < RING else G_FF + before[j]
                    split(u, 16 * (u // RING + 1), u + 1, freed)
                    if j == 0:
                        lows(1, 0)
                        lows(1, 1)
                    elif j == 1:
                        lows(1, 2)
                with pool.Fori(1, FPAIRS) as i:
                    for j in range(FF_UNITS):
                        u = U_FF + j
                        split(u, i * (16 * FF_UNITS // RING) + 16 * (u // RING + 1),
                              i * FF_UNITS + (u + 1), i * FF_GROUPS + (G_FF + before[j]))

            @block.tensor
            def _(pe):
                def open_group(g):
                    if g >= ACCS:
                        pe.wait_ge(acc_free[g % ACCS], g // ACCS)

                def passes(out, slot, k, hi, lo, first, last):
                    wh = w_hi[:, slot, k * P:(k + 1) * P]
                    wl = w_lo[:, slot, k * P:(k + 1) * P]
                    nc.tensor.matmul(out, wh, hi, start=first, stop=False)
                    nc.tensor.matmul(out, wh, lo, start=False, stop=False)
                    return nc.tensor.matmul(out, wl, hi, start=False, stop=last)

                for s in STEPS:
                    if s[0] == "stat":
                        _, n, tt = s
                        g = GROUP[s]
                        open_group(g)
                        pe.wait_ge(set_up, 16)
                        pe.wait_ge(sq_added, ADDED[("square", n, tt, KC - 1)] + 1)
                        nc.tensor.matmul(bank(g)[:, 0:width(tt)], c_("ones"), sums[tt][:, 0:width(tt)],
                                         start=True, stop=True).then_inc(acc_full, 1)
                    elif s[0] == "z":
                        _, u, tt = s
                        g = GROUP[s]
                        open_group(g)
                        if tt == 0:
                            pe.wait_ge(w_ready, u + 1)
                        out = bank(g)[:, 0:width(tt)]
                        order = range(KC) if u < U_WO else [*range(GH, KC), *range(GH)]
                        for k in order:
                            if u == 0:
                                split_in(pe, tt, k)
                            if u == U_WO:
                                pe.wait_ge(o_ready, SPLIT[("split", k, tt)] + 1)
                            if u == U_GA:
                                both = w_lo[:, u % RING, k * P:k * P + 2 * RANK]
                                high = w_hi[:, u % RING, k * P:k * P + RANK]
                                nc.tensor.matmul(out[0:2 * RANK], both, h_hi[:, k, cols(tt)], start=k == 0,
                                                 stop=k == KC - 1, skip_group_check=True)
                                last = nc.tensor.matmul(out[0:RANK], high, h_lo[:, k, cols(tt)], start=False,
                                                        stop=k == KC - 1, skip_group_check=True)
                                continue
                            last = passes(out, u % RING, k, h_hi[:, k, cols(tt)], h_lo[:, k, cols(tt)],
                                          k == order[0], k == order[-1])
                        last.then_inc(acc_full, 1)
                    elif s[0] == "turn_v":
                        _, u, tt = s
                        g = GROUP[s]
                        open_group(g)
                        left(pe, GROUP[("z", u, tt)])
                        n_done = count_before(STEPS, "turn_v", s)
                        for j in range(3):
                            w = NS if tt == NTT - 1 and j == 2 else P
                            last = nc.tensor.transpose(bank(g)[0:w, j * P:(j + 1) * P],
                                                       tmp_a[:, n_done % 2, j * P:j * P + w], c_("ident"))
                        last.then_inc(acc_full, 1)
                    elif s[0] == "turn_k":
                        g = GROUP[s]
                        open_group(g)
                        pe.wait_ge(roped, NTT)
                        nc.tensor.transpose(bank(g)[:, 0:P], ks[:, SEQ - P:SEQ], c_("ident"))
                        nc.tensor.transpose(bank(g)[0:NS, P:2 * P], ks[:, SEQ:T],
                                            c_("ident")).then_inc(acc_full, 1)
                    elif s[0] == "gate":
                        _, p, tt = s
                        g = GROUP[s]
                        open_group(g)
                        left(pe, GROUP[("z", U_GA, tt)])
                        pe.wait_ge(gk2_loaded, 32)
                        nc.tensor.matmul(bank(g)[:, 0:width(tt)], gk2[:, p * P:(p + 1) * P],
                                         gat[:, tt % 2, 0:width(tt)], start=True, stop=True).then_inc(acc_full, 1)
                    elif s[0] == "dec_scores":
                        _, g = s
                        r = slice(64 * g, 64 * g + 64)
                        if g == 0:
                            pe.wait_ge(dq_packed, 1)
                            pe.wait_ge(loaded, 16 * 3)
                        else:
                            pe.wait_ge(sc_read, g)
                            pe.wait_ge(pv_copied, g)
                        q = dq[r, :]
                        for b in range(2):
                            nc.tensor.matmul(pair_a[:, 512 * b:512 * b + 512], q, kct[r, 4 * b:4 * b + 4, :],
                                             start=True, stop=True)
                        nc.tensor.matmul(single[:, 0:NS], q, ks[r, SEQ:T], start=True,
                                         stop=True).then_inc(sc_full, 1)
                    elif s[0] == "dec_turn":
                        _, g = s
                        pe.wait_ge(p_norm, g + 1)
                        if g > 0:
                            pe.wait_ge(pt_copied, g)
                        for b in range(NB):
                            nc.tensor.transpose(pair_b[:, P * b:P * b + P], dprob[:, P * b:P * b + P], c_("ident"))
                        nc.tensor.transpose(single[0:NS, P:2 * P], dprob[:, SEQ:T],
                                            c_("ident")).then_inc(pt_full, 1)
                    elif s[0] == "dec_values":
                        _, g = s
                        r = slice(64 * g, 64 * g + 64)
                        pe.wait_ge(pt_copied, g + 1)
                        left(pe, GROUP[("turn_v", U_SV, NTT - 1)])
                        for b in range(NB):
                            nc.tensor.matmul(single[r, 256:384], vct[:, b, r], dprob_t[:, b, :],
                                             start=b == 0, stop=False)
                        nc.tensor.matmul(single[r, 256:384], sv[0:NS, 8, r], dnew_t[:, :],
                                         start=False, stop=True).then_inc(pv_full, 1)
                    elif s[0] == "scores":
                        n = s[1]
                        blk, g = n // 2, n % 2
                        r = slice(64 * g, 64 * g + 64)
                        lo = P if blk == 0 else 0
                        pe.wait_ge(sc_read, n + 2)
                        for hh in range(4):
                            last = nc.tensor.matmul(pair_a[:, 256 * hh + lo:256 * hh + 256],
                                                    qs[r, hh, blk * P:(blk + 1) * P],
                                                    ks[r, (blk - 1) * P + lo:(blk + 1) * P],
                                                    start=True, stop=True)
                        last.then_inc(sc_full, 1)
                    elif s[0] == "turn_p":
                        n = s[1]
                        blk = n // 2
                        pe.wait_ge(p_norm, n + 3)
                        pe.wait_ge(pt_copied, n + 2)
                        for kb in range(1 if blk == 0 else 0, 2):
                            for hh in range(4):
                                last = nc.tensor.transpose(pair_b[:, 512 * kb + P * hh:512 * kb + P * hh + P],
                                                           prob[:, n % 2, hh, P * kb:P * kb + P], c_("ident"))
                        last.then_inc(pt_full, 1)
                    elif s[0] == "values":
                        n = s[1]
                        blk, g = n // 2, n % 2
                        r = slice(64 * g, 64 * g + 64)
                        pe.wait_ge(pt_copied, n + 3)
                        pe.wait_ge(pv_copied, n + 2)
                        for kb in range(1 if blk == 0 else 0, 2):
                            last = nc.tensor.matmul(single[r, :], sv[:, blk - 1 + kb, r], prob_t[:, kb, :, :],
                                                    start=kb == (1 if blk == 0 else 0), stop=kb == 1)
                        last.then_inc(pv_full, 1)
                    elif s[0] == "gla_scores":
                        c = s[1]
                        pe.wait_ge(dec_mult, c + 1)
                        if c == 0:
                            pe.wait_ge(sc_read, 2 * NCH + 2)
                        else:
                            pe.wait_ge(ga_masked, c)
                        scores = pair_a[:, 0:GH * P].rearrange("p (q h n) -> p q h n", q=PAIRS, h=2)
                        for p in range(PAIRS):
                            for i in range(NSUB):
                                a = (p * NSUB + i) * P
                                last = nc.tensor.matmul(scores[:, p, :, i * SUB:(i + 1) * SUB],
                                                        edec[:, c % 2, a:a + P], qpad[p][:, i, :, :],
                                                        start=True, stop=True)
                        last.then_inc(ga_full, 1)
                    elif s[0] == "gla_turn":
                        c = s[1]
                        if c == 0:
                            pe.wait_ge(pt_copied, 2 * NCH + 2)
                            left(pe, GROUP[("turn_v", U_GG - 1, NTT - 1)])
                        else:
                            pe.wait_ge(kd_copied, c)
                        for p in range(PAIRS):
                            a = 1280 + p * P
                            last = nc.tensor.transpose(pair_b[:, p * P:(p + 1) * P], edec[:, c % 2, a:a + P],
                                                       c_("ident"))
                        last.then_inc(kd_turned, 1)
                    elif s[0] == "gla_state":
                        c = s[1]
                        pe.wait_ge(kd_copied, c + 1)
                        if c > 0:
                            pe.wait_ge(s_ready, c)
                        for hd in range(GH):
                            p, r = hd // 2, slice(64 * (hd % 2), 64 * (hd % 2) + 64)
                            last = nc.tensor.matmul(pair_b[r, 512 + p * P:512 + (p + 1) * P],
                                                    kdn[:, c % 2, p, r], vo[:, c, hd, :], start=True, stop=True)
                        last.then_inc(ds_full, 1)
                    elif s[0] == "gla_out":
                        c = s[1]
                        pe.wait_ge(ga_masked, c + 1)
                        if c == 0:
                            pe.wait_ge(pv_copied, 2 * NCH + 2)
                        else:
                            pe.wait_ge(go_copied, c)
                            pe.wait_ge(s_ready, c)
                        for hd in range(GH):
                            last = nc.tensor.matmul(single[:, hd * P:(hd + 1) * P], vo[:, c, hd, :],
                                                    asb[:, c % 2, hd, :], start=True, stop=c == 0)
                            if c > 0:
                                last = nc.tensor.matmul(single[:, hd * P:(hd + 1) * P], st[:, hd, :],
                                                        qh[:, c % 2, hd // 2, :], start=False, stop=True)
                        last.then_inc(go_full, 1)
                    elif s[0] == "gla_stat":
                        c = s[1]
                        g = GROUP[s]
                        open_group(g)
                        w = P if c < NCH else NS
                        pe.wait_ge(gn_square, c + 1)
                        nc.tensor.matmul(bank(g)[:, 0:GH * w], c_("ones"), gsq[:, 0:GH * w],
                                         start=True, stop=True).then_inc(acc_full, 1)
                    elif s[0] == "sample_scores":
                        pe.wait_ge(dec_mult, NCH + 1)
                        pe.wait_ge(ga_masked, NCH)
                        for hd in range(GH):
                            p, r = hd // 2, slice(64 * (hd % 2), 64 * (hd % 2) + 64)
                            last = nc.tensor.matmul(pair_a[0:NS, 512 * (hd % 2) + p * NS:512 * (hd % 2) + (p + 1) * NS], esam[r, 0, p, :],
                                                    qh[r, 0, p, 0:NS], start=True, stop=True)
                        last.then_inc(ga_full, 1)
                        pe.wait_ge(s_ready, NCH)
                        for p in range(PAIRS):
                            last = nc.tensor.transpose(pair_b[0:NS, p * P:(p + 1) * P], esam[:, 1, p, :],
                                                       c_("ident"))
                        last.then_inc(kd_turned, 1)
                    elif s[0] == "sample_out":
                        pe.wait_ge(ga_masked, NCH + 1)
                        pe.wait_ge(go_copied, NCH)
                        pe.wait_ge(s0_loaded, 32)
                        out_s = single[:, 0:GH * NS].rearrange("p (q h n) -> p q h n", q=PAIRS, h=2)
                        for p in range(PAIRS):
                            for h in range(2):
                                nc.tensor.matmul(out_s[:, p, h, :], vo[0:NS, NCH, 2 * p + h, :],
                                                 asam[:, 2 * p + h, :], start=p == 0 and h == 0, stop=False,
                                                 skip_group_check=True)
                        for p in range(PAIRS):
                            for b in range(NB):
                                t = slice(NT * b, NT * (b + 1))
                                last = nc.tensor.matmul(out_s[:, p, :, t], s0[:, b, p, :], qz[:, p, :, t],
                                                        start=False, stop=p == PAIRS - 1 and b == NB - 1,
                                                        skip_group_check=True)
                        last.then_inc(go_full, 1)
                    elif s[0] == "sample_states":
                        pe.wait_ge(kd_copied, NCH + 2)
                        pe.wait_ge(go_copied, NCH + 1)
                        for b in range(NB):
                            for hd in range(GH):
                                p, r = hd // 2, slice(64 * (hd % 2), 64 * (hd % 2) + 64)
                                dst = pair_a if b < 4 else pair_b
                                o = (b % 4) * 256 + p * P
                                last = nc.tensor.matmul(dst[r, o:o + P],
                                                        kdm[:, b, p * P + r.start:p * P + r.stop],
                                                        vo[0:NS, NCH, hd, :], start=True, stop=True)
                        last.then_inc(ds_full, 1)

                with pe.Fori(0, FPAIRS) as i:
                    def ff_open(j):
                        g = G_FF + j
                        pe.wait_ge(acc_free[g % ACCS], i * (FF_GROUPS // ACCS) + g // ACCS)
                        return bank(g)

                    for j in range(4):
                        u = U_FF + j
                        pe.wait_ge(w_ready, i * FF_UNITS + (u + 1))
                        for tt in range(NTT):
                            out = ff_open(NTT * j + tt)[:, 0:width(tt)]
                            for k in range(KC):
                                if j == 0:
                                    split_in(pe, NTT + tt, k)
                                last = passes(out, u % RING, k, h_hi[:, k, cols(tt)], h_lo[:, k, cols(tt)],
                                              k == 0, k == KC - 1)
                            last.then_inc(acc_full, 1)
                    for j in range(2):
                        u = U_FF + 4 + j
                        pe.wait_ge(w_ready, i * FF_UNITS + (u + 1))
                        for tt in range(NTT):
                            pe.wait_ge(hid_ready, i * (2 * NTT) + (NTT + tt + 1))
                            for d in range(4):
                                out = ff_open(4 * NTT + 4 * (NTT * j + tt) + d)[:, 0:width(tt)]
                                for f in range(2):
                                    last = passes(out, u % RING, 4 * f + d, hid_hi[:, f, cols(tt)],
                                                  hid_lo[:, f, cols(tt)], f == 0, f == 1)
                                last.then_inc(acc_full, 1)

            @block.scalar
            def _(act):
                chain = [0]

                def link(ins):
                    chain[0] += 1
                    ins.then_inc(act_chain, 1)
                    act.wait_ge(act_chain, chain[0])

                nc.scalar.preload_act_table_set(LN_EXP)

                for s in STEPS:
                    if s[0] == "square":
                        _, n, tt, k = s
                        w = width(tt)
                        if n == 0:
                            act.wait_ge(x_in[tt], 16)
                        else:
                            if SQUARE[s] == NTT * KC:
                                nc.scalar.preload_act_table_set(LN_EXP)
                                act.wait_ge(state_stored, 16 * GH)
                            left(act, GROUP[("z", U_WO + k, tt)])
                        if k == 0:
                            dst = sums[tt][:, 0:w]
                        else:
                            j = ADDED[s]
                            if j >= SQR:
                                act.wait_ge(sq_added, j - SQR + 1)
                            dst = sqr[:, j % SQR, 0:w]
                        nc.scalar.activation(dst, x[:, k, cols(tt)], ACT.Square).then_inc(squares, 1)
                    elif s[0] == "rstd":
                        _, n, tt = s
                        g = GROUP[("stat", n, tt)]
                        w = width(tt)
                        act.wait_ge(acc_full, g + 1)
                        if n == 0 and tt == 0:
                            act.wait_ge(set_up, 16)
                        nc.scalar.activation(rstds[:, tt, 0:w], bank(g)[:, 0:w], ACT.Ln, bias=c_("eps"),
                                             scale=1.0 / D_MODEL).then_inc(acc_free[g % ACCS], 1)
                        act.wait_ge(acc_free[g % ACCS], g // ACCS + 1)
                        nc.scalar.activation(rstds[:, tt, 0:w], rstds[:, tt, 0:w], ACT.Exp,
                                             scale=-0.5).then_inc(rstd_ready, 1)
                    elif s[0] == "normed":
                        _, n, tt, half = s
                        m = NTT * n + tt
                        if n == 1:
                            act.wait_ge(acc_full, GROUP[("z", U_FF - 1, tt)] + 1)
                        for k in range(KC // 2 * half, KC // 2 * (half + 1)):
                            act.wait_ge(hf_made, KC * m + k + 1)
                            nc.scalar.activation(h_hi[:, k, cols(tt)], tmp_n[:, k % 4, 0:width(tt)],
                                                 ACT.Copy).then_inc(hi_made, 1)
                    elif s[0] == "park":
                        act.dma_start(dmask[:], dec_mask).then_inc(loaded, 16)
                        act.dma_start(kct[:], kcache_t[layer]).then_inc(loaded, 16)
                        act.dma_start(vct[:], vcache[layer].rearrange("b t c -> t b c")).then_inc(loaded, 16)
                        act.dma_start(kc_s[layer, :, 0:WCACHE - NT, :],
                                      kcache[layer, :, NT:WCACHE, :]).then_inc(out_sem, 16)
                        act.dma_start(vc_s[layer, :, 0:WCACHE - NT, :],
                                      vcache[layer, :, NT:WCACHE, :]).then_inc(out_sem, 16)
                        act.wait_ge(hf_made, KC * NTT)
                        act.dma_start(park, x[:, GH:KC, :]).then_inc(parked, 16)
                    elif s[0] == "unpark":
                        act.wait_ge(sg_used, GH)
                        act.dma_start(x[:, GH:KC, :], park).then_inc(unparked, 16)
                    elif s[0] == "take":
                        _, u, tt = s
                        g = GROUP[("z", u, tt)]
                        w = width(tt)
                        b = bank(g)
                        if u == U_SV or U_GV <= u < U_GG:
                            act.wait_ge(acc_full, g + 1)
                            n_done = count_before(STEPS, "turn_v", ("turn_v", u, tt))
                            if u == U_SV and tt < 2:
                                split_in(act, NTT - 1, DVE_LOWS[-1])
                                split_in(act, NTT - 1, POOL_LOWS[-1])
                            nc.scalar.activation(tmp_a[:, n_done % 2, 0:w], b[:, 0:w], ACT.Copy)\
                              .then_inc(acc_free[g % ACCS], 1)
                        elif U_GK <= u < U_GA:
                            act.wait_ge(acc_full, g + 1)
                            dst = (kg if u < U_GQ else qg)[:, (u - U_GK) % 2, cols(tt)]
                            nc.scalar.activation(dst, b[:, 0:w], ACT.Copy, scale=1.0 if u < U_GQ else 0.125)\
                              .then_inc(acc_free[g % ACCS], 1)
                        elif u == U_GA:
                            act.wait_ge(acc_full, g + 1)
                            if tt == 2:
                                act.wait_ge(acc_full, GROUP[("gate", PAIRS - 1, 0)] + 1)
                            nc.scalar.activation(gat[:, tt % 2, 0:w], b[0:2 * RANK, 0:w], ACT.Copy)\
                              .then_inc(acc_free[g % ACCS], 1)
                        elif U_GG <= u < U_WO:
                            act.wait_ge(acc_full, g + 1)
                            act.wait_ge(parked, 16)
                            nc.scalar.activation(x[:, GH + u - U_GG, cols(tt)], b[:, 0:w], ACT.Copy)\
                              .then_inc(acc_free[g % ACCS], 1)
                    elif s[0] == "turn_v":
                        _, u, tt = s
                        g = GROUP[s]
                        act.wait_ge(acc_full, g + 1)
                        b3 = bank(g)[:, 0:3 * P].rearrange("p (j n) -> p j n", j=3)
                        nj = 3 if tt < NTT - 1 else 2
                        if u == U_SV:
                            dst, new = sv[:, 3 * tt:3 * tt + nj, :], sv[0:NS, 8, :]
                        else:
                            if u == U_GV and tt == 0:
                                act.wait_ge(pv_full, 2)
                                act.wait_ge(out_sem, 16 * (4 + 2 * NB))
                            hd = u - U_GV
                            dst, new = vo[:, 3 * tt:3 * tt + nj, hd, :], vo[0:NS, 8, hd, :]
                        last = nc.scalar.activation(dst, b3[:, 0:nj, :], ACT.Copy)
                        if tt == NTT - 1:
                            last = nc.scalar.activation(new, bank(g)[0:NS, 2 * P:3 * P], ACT.Copy)
                        last.then_inc(acc_free[g % ACCS], 1)
                    elif s[0] == "turn_k":
                        g = GROUP[s]
                        act.wait_ge(acc_full, g + 1)
                        nc.scalar.activation(kno[:, 0, :], bank(g)[:, 0:P], ACT.Copy)
                        nc.scalar.activation(kno[0:NS, 1, :], bank(g)[0:NS, P:2 * P], ACT.Copy)\
                          .then_inc(acc_free[g % ACCS], 1)
                        act.wait_ge(acc_free[g % ACCS], g // ACCS + 1)
                        act.dma_start(kc_p[layer, 0], kno[:, 0, :]).then_inc(out_sem, 16)
                        act.dma_start(vc_p[layer, 0], sv[:, NCH - 1, :]).then_inc(out_sem, 16)
                        for b in range(NB):
                            r = slice(NT * b, NT * (b + 1))
                            act.dma_start(kc_s[layer, b, WCACHE - NT:WCACHE, :], kno[r, 1, :]).then_inc(out_sem, 16)
                            act.dma_start(vc_s[layer, b, WCACHE - NT:WCACHE, :], sv[r, 8, :]).then_inc(out_sem, 16)
                    elif s[0] == "gate":
                        _, p, tt = s
                        g = GROUP[s]
                        w = width(tt)
                        n_done = PAIRS * tt + p
                        act.wait_ge(acc_full, g + 1)
                        ga, gb = sqt[:, n_done % 2, 0:w], tmp_b[:, n_done % 2, 0:w]
                        if n_done > 1:
                            act.wait_ge(gates_ready, n_done - 1)
                        if n_done == 0:
                            act.wait_ge(par_loaded, 16)
                            act.wait_ge(roped, 5 * NTT)
                        nc.scalar.activation(ga, bank(g)[:, 0:w], ACT.Identity,
                                             bias=p_("b_gate", p)).then_inc(acc_free[g % ACCS], 1)
                        act.wait_ge(acc_free[g % ACCS], g // ACCS + 1)
                        link(nc.scalar.activation(gb, ga, ACT.Abs))
                        link(nc.scalar.activation(gb, gb, ACT.Exp, scale=-1.0))
                        nc.scalar.activation(gb, gb, ACT.Ln, bias=1.0)\
                          .then_inc(gate_log, 1)
                    elif s[0] in ("dec_scores", "exp_p"):
                        n = s[1]
                        if s[0] == "dec_scores":
                            act.wait_ge(max_ready, n + 1)
                            nc.scalar.activation(small[:, 3:4], small[:, 2:3], ACT.Exp)
                            nc.scalar.activation(dprob[:], dprob[:], ACT.Exp, bias=small[:, 1:2],
                                                 accum_out=small[:, 4:5]).then_inc(p_exp, 1)
                        else:
                            lo = P if n < 2 else 0
                            o = 24 * (n % 2)
                            act.wait_ge(max_ready, n + 3)
                            nc.scalar.activation(small[:, o + 12:o + 16], small[:, o + 8:o + 12], ACT.Exp)
                            for hh in range(4):
                                pr = prob[:, n % 2, hh, lo:256]
                                last = nc.scalar.activation(pr, pr, ACT.Exp, bias=small[:, o + 4 + hh:o + 5 + hh],
                                                            accum_out=small[:, o + 16 + hh:o + 17 + hh])
                            last.then_inc(p_exp, 1)
                    elif s[0] == "dec_turn":
                        _, g = s
                        act.wait_ge(pt_full, g + 1)
                        if g > 0:
                            act.wait_ge(pv_full, g)
                        nc.scalar.activation(dprob_t[:], pair_b[:].rearrange("p (b n) -> p b n", b=NB), ACT.Copy)
                        nc.scalar.activation(dnew_t[:], single[0:NS, P:2 * P], ACT.Copy).then_inc(pt_copied, 1)
                    elif s[0] == "turn_p":
                        n = s[1]
                        k0 = 1 if n < 2 else 0
                        act.wait_ge(pt_full, n + 3)
                        act.wait_ge(pv_full, n + 2)
                        nc.scalar.activation(prob_t[:, k0:2, :, :],
                                             pair_b[:, 512 * k0:1024].rearrange("p (a h n) -> p a h n", h=4, n=P),
                                             ACT.Copy).then_inc(pt_copied, 1)
                    elif s[0] in ("dec_values", "values"):
                        if s[0] == "dec_values":
                            g = s[1]
                            r = slice(64 * g, 64 * g + 64)
                            act.wait_ge(pv_full, g + 1)
                            nc.scalar.activation(qs[r, :, SEQ:T],
                                                 single[r, 256:384].rearrange("p (h n) -> p h n", h=4),
                                                 ACT.Copy).then_inc(pv_copied, 1)
                        else:
                            n = s[1]
                            blk, g = n // 2, n % 2
                            r = slice(64 * g, 64 * g + 64)
                            act.wait_ge(pv_full, n + 3)
                            nc.scalar.activation(qs[r, :, blk * P:(blk + 1) * P],
                                                 single[r, :].rearrange("p (h n) -> p h n", h=4),
                                                 ACT.Copy).then_inc(pv_copied, 1)
                            if n == 2 * NCH - 1:
                                act.wait_ge(out_sem, 16 * (4 + 2 * NB))
                                for b in range(0, NB, 4):
                                    act.dma_start(s0[:, b:b + 4], state_in[layer, b:b + 4].rearrange(
                                        "b (q r) v -> r b q v", r=P)).then_inc(s0_loaded, 16)
                    elif s[0] == "gla_exps":
                        c = s[1]
                        cc = slice(c * P, (c + 1) * P)
                        act.wait_ge(gates_ready, PAIRS * NTT)
                        if c >= 2:
                            act.wait_ge(s_ready, c - 1)
                            act.wait_ge(go_full, c - 1)
                        nc.scalar.activation(qh[:, c % 2, :, :], bg[:, :, cc], ACT.Exp, scale=1.0 / GATE_NORM)
                        act.wait_ge(dec_ready, c + 1)
                        nc.scalar.activation(edec[:, c % 2, :], edec[:, c % 2, :], ACT.Exp,
                                             scale=1.0 / GATE_NORM).then_inc(dec_exp, 1)
                    elif s[0] == "gla_turn":
                        c = s[1]
                        act.wait_ge(kd_turned, c + 1)
                        nc.scalar.activation(kdn[:, c % 2, :, :],
                                             pair_b[:, 0:PAIRS * P].rearrange("p (q n) -> p q n", q=PAIRS),
                                             ACT.Copy).then_inc(kd_copied, 1)
                    elif s[0] == "gla_out":
                        c = s[1]
                        act.wait_ge(go_full, c + 1)
                        nc.scalar.activation(vo[:, c, :, :], single[:].rearrange("p (h n) -> p h n", h=GH),
                                             ACT.Copy).then_inc(go_copied, 1)
                    elif s[0] == "gla_state_sum":
                        if s[1] == NCH - 1:
                            act.wait_ge(s_ready, NCH)
                            for hd in range(GH):
                                r = slice(64 * (hd % 2), 64 * (hd % 2) + 64)
                                act.dma_start(state_p[layer, 0, 64 * hd:64 * hd + 64], st[r, hd, :])\
                                   .then_inc(state_stored, 16)
                    elif s[0] == "gla_square":
                        c = s[1]
                        w = P if c < NCH else NS
                        act.wait_ge(go_copied, c + 1)
                        if c > 0:
                            act.wait_ge(acc_full, GROUP[("gla_stat", c - 1)] + 1)
                        sq3 = gsq[:, 0:GH * w].rearrange("p (h n) -> p h n", h=GH)
                        nc.scalar.activation(sq3, vo[:, c, :, :] if c < NCH else o_s[:],
                                             ACT.Square).then_inc(gn_square, 1)
                    elif s[0] == "gla_rstd":
                        c = s[1]
                        g = GROUP[("gla_stat", c)]
                        w = P if c < NCH else NS
                        act.wait_ge(acc_full, g + 1)
                        if c > 0:
                            act.wait_ge(gn_done, c)
                        nc.scalar.activation(grstd[:, 0:GH * w], bank(g)[:, 0:GH * w], ACT.Ln, bias=c_("eps"),
                                             scale=1.0 / P).then_inc(acc_free[g % ACCS], 1)
                        act.wait_ge(acc_free[g % ACCS], g // ACCS + 1)
                        nc.scalar.activation(grstd[:, 0:GH * w], grstd[:, 0:GH * w], ACT.Exp,
                                             scale=-0.5).then_inc(gn_rstd, 1)
                    elif s[0] == "sample_exps":
                        act.wait_ge(go_full, NCH - 1)
                        nc.scalar.activation(qh[:, 0, :, 0:NS], bg[:, :, SEQ:T], ACT.Exp, scale=1.0 / GATE_NORM)
                        act.wait_ge(dec_ready, NCH + 1)
                        nc.scalar.activation(esam[:], esam[:], ACT.Exp, scale=1.0 / GATE_NORM).then_inc(dec_exp, 1)
                    elif s[0] == "sample_scores":
                        act.wait_ge(kd_turned, NCH + 1)
                        nc.scalar.activation(kdn[0:NS, 0, :, :],
                                             pair_b[0:NS, 0:PAIRS * P].rearrange("p (q n) -> p q n", q=PAIRS),
                                             ACT.Copy).then_inc(kd_copied, 1)
                    elif s[0] == "sample_out":
                        act.wait_ge(go_full, NCH + 1)
                        nc.scalar.activation(o_s[:], single[:, 0:GH * NS].rearrange("p (h n) -> p h n", h=GH),
                                             ACT.Copy).then_inc(go_copied, 1)
                    elif s[0] == "silu":
                        hd = s[1]
                        gx = x[:, GH + hd, :]
                        left(act, GROUP[("z", U_GG + hd, NTT - 1)])
                        nc.scalar.activation(gx, gx, ACT.Silu).then_inc(silu_made, 1)
                    elif s[0] == "split":
                        _, k, tt = s
                        nj = 3 if tt < NTT - 1 else 2
                        c0 = COLS[tt][0]
                        act.wait_ge(acc_full, GROUP[("z", U_WO - 1, tt)] + 1)
                        if SPLIT[s] == 0:
                            act.wait_ge(pv_copied, 2 * NCH + 2)
                        if k < GH:
                            act.wait_ge(sg_used, k + 1)
                            dst = h_hi[:, k, c0:c0 + nj * P].rearrange("p (j n) -> p j n", j=nj)
                            last = nc.scalar.activation(dst, vo[:, 3 * tt:3 * tt + nj, k, :], ACT.Copy)
                            if tt == NTT - 1:
                                last = nc.scalar.activation(h_hi[:, k, SEQ:T], o_s[:, k, :], ACT.Copy)
                        else:
                            last = nc.scalar.activation(h_hi[:, k, cols(tt)], qs[:, k - GH, cols(tt)], ACT.Copy)
                        last.then_inc(o_high, 1)
                with act.Fori(0, FPAIRS) as i:
                    for f in range(2):
                        for tt in range(NTT):
                            w = width(tt)
                            j = 2 * NTT * f + tt
                            g = G_FF + j
                            n_done = NTT * f + tt
                            act.wait_ge(acc_full, i * FF_GROUPS + (g + 1))
                            nc.scalar.activation(silu_g[:, tt, 0:w], bank(g)[:, 0:w], ACT.Silu)\
                              .then_inc(acc_free[g % ACCS], 1)
                        for tt in range(NTT):
                            w = width(tt)
                            n_done = NTT * f + tt
                            g = G_FF + NTT * (2 * f + 1) + tt
                            act.wait_ge(acc_free[g % ACCS], i * (FF_GROUPS // ACCS) + (g // ACCS + 1))
                            nc.scalar.activation(hid_hi[:, f, cols(tt)], tmp_a[:, n_done % 2, 0:w],
                                                 ACT.Copy).then_inc(hid_high, 1)
                act.wait_ge(out_sem, 16 * (5 + 2 * NB))

            @block.vector
            def _(dve):
                chain = [0]

                def link(ins):
                    chain[0] += 1
                    ins.then_inc(dve_chain, 1)
                    dve.wait_ge(dve_chain, chain[0])

                for s in STEPS:
                    if s[0] == "square":
                        _, n, tt, k = s
                        w = width(tt)
                        if s in ADDED:
                            dve.wait_ge(squares, SQUARE[s] + 1)
                            if ADDED[s] > 0:
                                dve.wait_ge(sq_added, ADDED[s])
                            nc.vector.tensor_tensor(sums[tt][:, 0:w], sums[tt][:, 0:w],
                                                    sqr[:, ADDED[s] % SQR, 0:w], ALU.add).then_inc(sq_added, 1)
                    elif s[0] == "normed":
                        _, n, tt, half = s
                        m = NTT * n + tt
                        w = width(tt)
                        k0, k1 = KC // 2 * half, KC // 2 * (half + 1)
                        dve.wait_ge(rstd_ready, m + 1)
                        dve.wait_ge(par_loaded, 16)
                        if n == 1:
                            dve.wait_ge(acc_full, GROUP[("z", U_FF - 1, tt)] + 1)
                        gain = "g_attn" if n == 0 else "g_ffn"
                        for k in range(k0, k1 + 1):
                            if k < k1:
                                if KC * m + k >= 4:
                                    split_in(dve, m + (k - 4) // KC, (k - 4) % KC)
                                if n == 0 and tt == 2 and k == 2:
                                    dve.wait_ge(roped, 1)
                                nc.vector.scalar_tensor_tensor(
                                    tmp_n[:, k % 4, 0:w], x[:, k, cols(tt)], p_(gain, k), rstds[:, tt, 0:w],
                                    ALU.mult, ALU.mult).then_inc(hf_made, 1)
                            if k > k0 and k - 1 in DVE_LOWS:
                                dve.wait_ge(hi_made, KC * m + k)
                                nc.vector.tensor_tensor(h_lo[:, k - 1, cols(tt)], tmp_n[:, (k - 1) % 4, 0:w],
                                                        h_hi[:, k - 1, cols(tt)].bitcast(f32),
                                                        ALU.subtract).then_inc(h_ready, 1)
                    elif s[0] == "take":
                        _, u, tt = s
                        g = GROUP[("z", u, tt)]
                        w = width(tt)
                        b = bank(g)
                        if u == U_SK or U_SQ <= u < U_SQ + 4:
                            dst = ks[:, cols(tt)] if u == U_SK else qs[:, u - U_SQ, cols(tt)]
                            dve.wait_ge(acc_full, g + 1)
                            if u == U_SK and tt == 0:
                                dve.wait_ge(rope_loaded, 16)
                            if u == U_SK:
                                split_in(dve, min(tt + 1, NTT - 1), POOL_LOWS[-1])
                                split_in(dve, min(tt + 1, NTT - 1), DVE_LOWS[-1])
                            turn = tt if u == U_SK else NTT * (1 + u - U_SQ) + tt
                            if turn > 0:
                                dve.wait_ge(roped, turn)
                            for a in range(4):
                                o = 32 * (a ^ 1)
                                nc.vector.tensor_tensor(tmp_b[32 * a:32 * a + 32, 0, 0:w], b[o:o + 32, 0:w],
                                                        rope[32 * a:32 * a + 32, 1, cols(tt)], ALU.mult)
                            nc.vector.tensor_tensor(tmp_b[:, 1, 0:w], b[:, 0:w], rope[:, 0, cols(tt)],
                                                    ALU.mult).then_inc(acc_free[g % ACCS], 1)
                            dve.wait_ge(acc_free[g % ACCS], g // ACCS + 1)
                            nc.vector.tensor_tensor(dst, tmp_b[:, 0, 0:w], tmp_b[:, 1, 0:w],
                                                    ALU.add).then_inc(roped, 1)
                        elif u >= U_WO:
                            dve.wait_ge(acc_full, g + 1)
                            if u - U_WO >= GH:
                                dve.wait_ge(unparked, 16)
                            xs = x[:, u - U_WO, cols(tt)]
                            nc.vector.tensor_tensor(xs, xs, b[:, 0:w], ALU.add).then_inc(acc_free[g % ACCS], 1)
                    elif s[0] == "gate":
                        _, p, tt = s
                        w = width(tt)
                        n_done = PAIRS * tt + p
                        dve.wait_ge(gate_log, n_done + 1)
                        ga, gb = sqt[:, n_done % 2, 0:w], tmp_b[:, n_done % 2, 0:w]
                        link(nc.vector.scalar_tensor_tensor(ga, ga, 0.0, gb, ALU.min, ALU.subtract))
                        c0 = COLS[tt][0]
                        for j in range(3 if tt < NTT - 1 else 2):
                            last = nc.vector.tensor_tensor_scan(
                                bg[:, p, c0 + j * P:c0 + (j + 1) * P], c_("ones"),
                                ga[:, j * P:(j + 1) * P], 0.0, ALU.mult, ALU.add)
                        if tt == NTT - 1:
                            last = nc.vector.tensor_tensor_scan(bg[:, p, SEQ:T], c_("reset"),
                                                                ga[:, 2 * P:2 * P + NS], 0.0,
                                                                ALU.mult, ALU.add)
                        last.then_inc(gates_ready, 1)
                    elif s[0] == "dec_scores":
                        _, g = s
                        if g == 0:
                            a = PO["sink"][0]
                            link(nc.vector.tensor_scalar(nsink, par[:, a:a + 10], -1.0, None, ALU.mult))
                            dve.wait_ge(roped, 5 * NTT)
                            dve.wait_ge(loaded, 16 * 3)
                            nc.vector.tensor_copy(dq[:].rearrange("p (h n) -> p h n", h=4),
                                                  qs[:, :, SEQ:T]).then_inc(dq_packed, 1)
                        dve.wait_ge(sc_full, g + 1)
                        if g > 0:
                            dve.wait_ge(pt_full, g)
                        nc.vector.scalar_tensor_tensor(dprob[:, 0:1024], pair_a[:], 0.125, dmask[:, 0:1024],
                                                       ALU.mult, ALU.add)
                        nc.vector.scalar_tensor_tensor(dprob[:, SEQ:T], single[:, 0:NS], 0.125, dmask[:, SEQ:T],
                                                       ALU.mult, ALU.add).then_inc(sc_read, 1)
                        dve.wait_ge(sc_read, g + 1)
                        link(nc.vector.tensor_reduce(small[:, 0:1], dprob[:], AX.X, ALU.max, negate=True))
                        link(nc.vector.tensor_tensor(small[:, 1:2], small[:, 0:1], nsink[:, 8 + g:9 + g], ALU.min))
                        nc.vector.tensor_tensor(small[:, 2:3], small[:, 1:2], p_("sink_rows", g),
                                                ALU.add).then_inc(max_ready, 1)
                    elif s[0] == "dec_norm":
                        _, g = s
                        dve.wait_ge(p_exp, g + 1)
                        link(nc.vector.tensor_tensor(small[:, 5:6], small[:, 3:4], small[:, 4:5], ALU.add))
                        link(nc.vector.reciprocal(small[:, 6:7], small[:, 5:6]))
                        nc.vector.tensor_scalar(dprob[:], dprob[:], small[:, 6:7], None, ALU.mult).then_inc(p_norm, 1)
                    elif s[0] == "scores":
                        n = s[1]
                        blk, g = n // 2, n % 2
                        lo = P if blk == 0 else 0
                        o = 24 * (n % 2)
                        pr = prob[:, n % 2, :, lo:256]
                        sc = pair_a[:].rearrange("p (h n) -> p h n", h=4)[:, :, lo:256]
                        band = c_("band")[:, lo:256].unsqueeze(1).broadcast_to([P, 4, 256 - lo])
                        dve.wait_ge(sc_full, n + 3)
                        dve.wait_ge(pt_full, max(n - 2 + 3, 2))
                        nc.vector.scalar_tensor_tensor(pr, sc, 0.125, band, ALU.mult, ALU.add).then_inc(sc_read, 1)
                        dve.wait_ge(sc_read, n + 3)
                        link(nc.vector.tensor_reduce(small[:, o:o + 4], pr, AX.X, ALU.max, negate=True))
                        link(nc.vector.tensor_tensor(small[:, o + 4:o + 8], small[:, o:o + 4],
                                                     nsink[:, 4 * g:4 * g + 4], ALU.min))
                        nc.vector.tensor_tensor(small[:, o + 8:o + 12], small[:, o + 4:o + 8],
                                                p_("sink", 4 * g, 4), ALU.add).then_inc(max_ready, 1)
                    elif s[0] == "norm_p":
                        n = s[1]
                        lo = P if n < 2 else 0
                        o = 24 * (n % 2)
                        pr = prob[:, n % 2, :, lo:256]
                        dve.wait_ge(p_exp, n + 3)
                        link(nc.vector.tensor_tensor(small[:, o + 16:o + 20], small[:, o + 12:o + 16],
                                                     small[:, o + 16:o + 20], ALU.add))
                        link(nc.vector.reciprocal(small[:, o + 20:o + 24], small[:, o + 16:o + 20]))
                        rec = small[:, o + 20:o + 24].unsqueeze(2).broadcast_to([P, 4, 256 - lo])
                        nc.vector.tensor_tensor(pr, pr, rec, ALU.mult).then_inc(p_norm, 1)
                    elif s[0] == "gla_exponents":
                        c = s[1]
                        cc = slice(c * P, (c + 1) * P)
                        e = edec[:, c % 2, :]
                        if c == 0:
                            left(dve, GROUP[("turn_v", U_GG - 1, NTT - 1)])
                            dve.wait_ge(pv_full, 2 * NCH + 2)
                            dve.wait_ge(gates_ready, PAIRS * NTT)
                        if c >= 2:
                            dve.wait_ge(ga_full, c - 1)
                            dve.wait_ge(kd_turned, c - 1)
                        b3 = bg[:, :, cc]
                        ref = b3.rearrange("p q (i n) -> p q i n", i=NSUB)[:, :, :, SUB // 2 - 1:SUB // 2]
                        for p in range(PAIRS):
                            nc.vector.tensor_tensor(
                                e[:, 512 * p:512 * p + 512].rearrange("p (i n) -> p i n", i=NSUB),
                                ref[:, p].broadcast_to([P, NSUB, P]),
                                b3[:, p].unsqueeze(1).broadcast_to([P, NSUB, P]), ALU.subtract)
                        link(nc.vector.tensor_tensor(
                            e[:, 1024:1280].rearrange("p (q i n) -> p q i n", q=PAIRS, i=NSUB),
                            b3.rearrange("p q (i n) -> p q i n", i=NSUB),
                            ref.broadcast_to([P, PAIRS, NSUB, SUB]), ALU.subtract))
                        nc.vector.tensor_scalar(e[:, 0:1280], e[:, 0:1280], CLAMP, None, ALU.min)
                        nc.vector.tensor_tensor(
                            e[:, 1280:1536].rearrange("p (q n) -> p q n", q=PAIRS),
                            b3[:, :, P - 1:P].broadcast_to([P, PAIRS, P]), b3, ALU.subtract).then_inc(dec_ready, 1)
                    elif s[0] == "gla_decays":
                        c = s[1]
                        cc = slice(c * P, (c + 1) * P)
                        e = edec[:, c % 2, :]
                        dve.wait_ge(dec_exp, c + 1)
                        if c > 1:
                            dve.wait_ge(s_ready, c - 1)
                        for p in range(PAIRS):
                            ek = e[:, 512 * p:512 * p + 512].rearrange("p (i n) -> p i n", i=NSUB)
                            nc.vector.tensor_tensor(ek, ek, kg[:, p, cc].unsqueeze(1).broadcast_to([P, NSUB, P]),
                                                    ALU.mult)
                        if c > 0:
                            dve.wait_ge(ga_full, c)
                        else:
                            nc.vector.memset(qpad[0][:], 0.0)
                            link(nc.vector.memset(qpad[1][:], 0.0))
                        for p in range(PAIRS):
                            for h in range(2):
                                r = slice(64 * h, 64 * h + 64)
                                o = 1024 + p * P
                                nc.vector.tensor_tensor(
                                    qpad[p][r, :, h, :], e[r, o:o + P].rearrange("p (i n) -> p i n", i=NSUB),
                                    qg[r, p, cc].rearrange("p (i n) -> p i n", i=NSUB), ALU.mult)
                        ed = e[:, 1280:1536].rearrange("p (q n) -> p q n", q=PAIRS)
                        nc.vector.tensor_tensor(ed, ed, kg[:, :, cc], ALU.mult)
                        k_ = 48 + 2 * (c % 2)
                        link(nc.vector.tensor_copy(small[:, k_:k_ + 2].unsqueeze(2), qh[:, c % 2, :, P - 1:P]))
                        nc.vector.tensor_tensor(qh[:, c % 2, :, :], qh[:, c % 2, :, :], qg[:, :, cc],
                                                ALU.mult).then_inc(dec_mult, 1)
                    elif s[0] == "gla_mask":
                        c = s[1]
                        dve.wait_ge(ga_full, c + 1)
                        if c >= 2:
                            dve.wait_ge(go_full, c - 1)
                        for hd in range(GH):
                            last = nc.vector.copy_predicated(asb[:, c % 2, hd, :], c_("causal").bitcast(u32),
                                                             pair_a[:, hd * P:(hd + 1) * P])
                        last.then_inc(ga_masked, 1)
                    elif s[0] == "gla_state_sum":
                        c = s[1]
                        dve.wait_ge(ds_full, c + 1)
                        if c > 0:
                            dve.wait_ge(go_full, c + 1)
                        if c > 0:
                            dve.wait_ge(s_ready, c)
                        else:
                            left(dve, GROUP[("gate", PAIRS - 1, NTT - 1)])
                            link(nc.vector.memset(st[:], 0.0))
                        for hd in range(GH):
                            p, r = hd // 2, slice(64 * (hd % 2), 64 * (hd % 2) + 64)
                            add = pair_b[r, 512 + p * P:512 + (p + 1) * P]
                            k_ = 48 + 2 * (c % 2) + p
                            if c == 0:
                                last = nc.vector.tensor_copy(st[r, hd, :], add)
                            else:
                                last = nc.vector.scalar_tensor_tensor(st[r, hd, :], st[r, hd, :],
                                                                      small[r, k_:k_ + 1], add,
                                                                      ALU.mult, ALU.add)
                        last.then_inc(s_ready, 1)
                    elif s[0] == "gla_scale":
                        c = s[1]
                        w = P if c < NCH else NS
                        dve.wait_ge(gn_rstd, c + 1)
                        o = vo[:, c, :, :] if c < NCH else o_s[:]
                        nc.vector.scalar_tensor_tensor(o, o, p_("g_gla"),
                                                       grstd[:, 0:GH * w].rearrange("p (h n) -> p h n", h=GH),
                                                       ALU.mult, ALU.mult).then_inc(gn_done, 1)
                    elif s[0] == "sample_exponents":
                        b3 = bg[:, :, SEQ:T]
                        b4 = b3.rearrange("p q (b t) -> p q b t", b=NB)
                        dve.wait_ge(kd_turned, NCH - 1)
                        dve.wait_ge(ga_full, NCH - 1)
                        nc.vector.memset(qz[:], 0.0)
                        link(nc.vector.memset(asam[:], 0.0))
                        nc.vector.tensor_scalar(esam[:, 0], b3, -1.0, CLAMP, ALU.mult, ALU.min)
                        nc.vector.tensor_tensor(esam[:, 1].rearrange("p q (b t) -> p q b t", b=NB),
                                                b4[:, :, :, NT - 1:NT].broadcast_to([P, PAIRS, NB, NT]), b4,
                                                ALU.subtract).then_inc(dec_ready, 1)
                    elif s[0] == "sample_decays":
                        dve.wait_ge(dec_exp, NCH + 1)
                        for e in range(2):
                            nc.vector.tensor_tensor(esam[:, e], esam[:, e], kg[:, :, SEQ:T], ALU.mult)
                        dec = qh[:, 0, :, 0:NS].rearrange("p q (b t) -> p b q t", b=NB)[:, :, :, NT - 1:NT]
                        keep = small[:, 0:16].rearrange("p (b q) -> p b q", b=NB)
                        link(nc.vector.tensor_copy(keep.unsqueeze(3), dec))
                        link(nc.vector.tensor_tensor(qh[:, 0, :, 0:NS], qh[:, 0, :, 0:NS], qg[:, :, SEQ:T],
                                                     ALU.mult))
                        for h in range(2):
                            r = slice(64 * h, 64 * h + 64)
                            last = nc.vector.tensor_copy(qz[r, :, h, :], qh[r, 0, :, 0:NS])
                        last.then_inc(dec_mult, 1)
                    elif s[0] == "sample_scores":
                        dve.wait_ge(ga_full, NCH + 1)
                        for hd in range(GH):
                            o = 512 * (hd % 2) + hd // 2 * NS
                            last = nc.vector.copy_predicated(asam[:, hd, :], c_("causal_s", NS).bitcast(u32),
                                                             pair_a[0:NS, o:o + NS])
                        last.then_inc(ga_masked, 1)
                        dve.wait_ge(kd_copied, NCH + 1)
                        for b in range(NB):
                            last = nc.vector.tensor_scalar(
                                kdm[:, b, :], kdn[0:NS, 0, :, :].rearrange("p q n -> p (q n)"),
                                c_("bmask", NS)[:, b:b + 1], None, ALU.mult)
                        last.then_inc(kd_copied, 1)
                    elif s[0] == "sample_sum":
                        keep = small[:, 0:16].rearrange("p (b q) -> p b q", b=NB)
                        dve.wait_ge(ds_full, NCH + 1)
                        dve.wait_ge(go_full, NCH + 1)
                        link(nc.vector.tensor_tensor(s0[:], s0[:], keep.unsqueeze(3).broadcast_to([P, NB, PAIRS, P]),
                                                     ALU.mult))
                        for half, src in ((0, pair_a), (1, pair_b)):
                            part = s0[:, 4 * half:4 * half + 4, :, :]
                            last = nc.vector.tensor_tensor(part, part,
                                                           src[:].rearrange("p (b q v) -> p b q v", b=4, q=PAIRS),
                                                           ALU.add)
                        last.then_inc(s_ready, 1)
                    elif s[0] == "gate_out":
                        hd = s[1]
                        dve.wait_ge(silu_made, hd + 1)
                        dve.wait_ge(gn_done, NCH + 1)
                        o = vo[:, 0:NCH, hd, :]
                        nc.vector.tensor_tensor(o, o, x[:, GH + hd, 0:SEQ].rearrange("p (j n) -> p j n", j=NCH),
                                                ALU.mult)
                        o = o_s[:, hd, :]
                        nc.vector.tensor_tensor(o, o, x[:, GH + hd, SEQ:T], ALU.mult).then_inc(sg_used, 1)
                    elif s[0] == "split":
                        _, k, tt = s
                        nj = 3 if tt < NTT - 1 else 2
                        c0 = COLS[tt][0]
                        dve.wait_ge(o_high, SPLIT[s] + 1)
                        if k < GH:
                            dve.wait_ge(sg_used, k + 1)
                            hi = h_hi[:, k, c0:c0 + nj * P].rearrange("p (j n) -> p j n", j=nj)
                            lo = h_lo[:, k, c0:c0 + nj * P].rearrange("p (j n) -> p j n", j=nj)
                            last = nc.vector.tensor_tensor(lo, vo[:, 3 * tt:3 * tt + nj, k, :],
                                                           hi.bitcast(f32), ALU.subtract)
                            if tt == NTT - 1:
                                last = nc.vector.tensor_tensor(h_lo[:, k, SEQ:T], o_s[:, k, :],
                                                               h_hi[:, k, SEQ:T].bitcast(f32), ALU.subtract)
                        else:
                            last = nc.vector.tensor_tensor(h_lo[:, k, cols(tt)], qs[:, k - GH, cols(tt)],
                                                           h_hi[:, k, cols(tt)].bitcast(f32), ALU.subtract)
                        last.then_inc(o_ready, 1)

                with dve.Fori(0, FPAIRS) as i:
                    for f in range(2):
                        for tt in range(NTT + 1):
                            if tt < NTT:
                                w = width(tt)
                                j = NTT * (2 * f + 1) + tt
                                g = G_FF + j
                                n_done = NTT * f + tt
                                gate = g - NTT
                                dve.wait_ge(acc_free[gate % ACCS], i * (FF_GROUPS // ACCS) + (gate // ACCS + 1))
                                dve.wait_ge(acc_full, i * FF_GROUPS + (g + 1))
                                if n_done >= 2:
                                    dve.wait_ge(hid_ready, i * (2 * NTT) + (n_done - 1))
                                else:
                                    b = G_FF - 1
                                    dve.wait_ge(acc_free[b % ACCS], i * (FF_GROUPS // ACCS) + (b // ACCS + 1))
                                nc.vector.tensor_tensor(tmp_a[:, n_done % 2, 0:w], silu_g[:, tt, 0:w],
                                                        bank(g)[:, 0:w], ALU.mult).then_inc(acc_free[g % ACCS], 1)
                            if tt > 0:
                                m = NTT * f + tt - 1
                                w = width(tt - 1)
                                dve.wait_ge(hid_high, i * (2 * NTT) + (m + 1))
                                nc.vector.tensor_tensor(hid_lo[:, f, cols(tt - 1)], tmp_a[:, m % 2, 0:w],
                                                        hid_hi[:, f, cols(tt - 1)].bitcast(f32),
                                                        ALU.subtract).then_inc(hid_ready, 1)
                    for j in range(2):
                        for tt in range(NTT):
                            for d in range(4):
                                g = G_FF + 4 * NTT + 4 * (NTT * j + tt) + d
                                dve.wait_ge(acc_full, i * FF_GROUPS + (g + 1))
                                xs = x[:, 4 * j + d, cols(tt)]
                                nc.vector.tensor_tensor(xs, xs, bank(g)[:, 0:width(tt)],
                                                        ALU.add).then_inc(acc_free[g % ACCS], 1)

        nc.sync.sem_clear(layer_sems)
        nc.all_engine_barrier()

    with nc.Block() as block:
        @block.scalar
        def _(act):
            nc.scalar.preload_act_table_set(LN_EXP)

            def root(tt):
                w = width(tt)
                act.wait_ge(fin["full"], KC * (tt + 1))
                nc.scalar.activation(rstds[:, tt, 0:w], acc[tt][:, 0:w], ACT.Ln, bias=c_("eps"),
                                     scale=1.0 / D_MODEL).then_inc(fin["ln"], 1)
                act.wait_ge(fin["ln"], tt + 1)
                nc.scalar.activation(rstds[:, tt, 0:w], rstds[:, tt, 0:w], ACT.Exp,
                                     scale=-0.5).then_inc(fin["rstd"], 1)

            for tt in range(NTT):
                for k in range(KC):
                    j = KC * tt + k
                    if j >= SQR:
                        act.wait_ge(fin["full"], j - SQR + 1)
                    nc.scalar.activation(sqr[:, j % SQR, 0:width(tt)], x[:, k, cols(tt)],
                                         ACT.Square).then_inc(fin["square"], 1)
                    if tt > 0 and k == SQR - 1:
                        root(tt - 1)
            root(NTT - 1)

        @block.tensor
        def _(pe):
            for tt in range(NTT):
                for k in range(KC):
                    j = KC * tt + k
                    pe.wait_ge(fin["square"], j + 1)
                    nc.tensor.matmul(acc[tt][:, 0:width(tt)], c_("ones"), sqr[:, j % SQR, 0:width(tt)],
                                     start=k == 0, stop=k == KC - 1).then_inc(fin["full"], 1)

        @block.vector
        def _(dve):
            dve.wait_ge(fin_in, 16)
            for tt in range(NTT):
                dve.wait_ge(fin["rstd"], tt + 1)
                for k in range(KC):
                    nc.vector.scalar_tensor_tensor(x[:, k, cols(tt)], x[:, k, cols(tt)], gfin[:, k:k + 1],
                                                   rstds[:, tt, 0:width(tt)], ALU.mult,
                                                   ALU.mult).then_inc(fin["out"], 1)

        @block.sync
        def _(sp):
            for tt in range(NTT):
                for half in range(2):
                    sp.wait_ge(fin["out"], KC * tt + KC // 2 * (half + 1))
                    kk = slice(KC // 2 * half, KC // 2 * (half + 1))
                    sp.dma_start(y_t[:, kk, cols(tt)], x[:, kk, cols(tt)]).then_inc(fin["stored"], 16)
            sp.wait_ge(fin["stored"], 16 * 2 * NTT)


def shape_constants(np):
    CO, n = offsets(CONSTS)
    const = np.zeros((P, n), np.float32)
    i = np.arange(P)
    const[:, slice(*CO["ident"])] = np.eye(P)
    const[:, slice(*CO["ones"])] = 1.0
    key = np.arange(256)[None] - P
    ok = (key <= i[:, None]) & (i[:, None] - key < WCACHE)
    const[:, slice(*CO["band"])] = np.where(ok, 0.0, NEG)
    const[:, slice(*CO["eps"])] = EPS
    j = np.arange(NS)
    const[:, slice(*CO["reset"])] = (j % NT != 0)[None]
    const[0:NS, slice(*CO["bmask"])] = j[:, None] // NT == np.arange(NB)[None]
    const[:, slice(*CO["causal"])] = i[:, None] <= i[None]
    const[0:NS, slice(*CO["causal_s"])] = (j[:, None] <= j[None]) & (j[:, None] // NT == j[None] // NT)
    row = np.arange(P)
    rb, rt = row % NS // NT, row % NT
    dec = np.full((P, T), NEG, np.float32)
    kb, kj = np.arange(SEQ) // WCACHE, np.arange(SEQ) % WCACHE
    dec[:, 0:SEQ][(kb[None] == rb[:, None]) & (kj[None] > rt[:, None])] = 0.0
    dec[:, SEQ:][(j[None] // NT == rb[:, None]) & (j[None] % NT <= rt[:, None])] = 0.0
    pos = np.concatenate([np.arange(SEQ), SEQ + j % NT]).astype(np.float32)
    half = 32
    inv = np.float32(10000.0) ** (-np.arange(half, dtype=np.float32) / np.float32(half))
    ang = (pos[None] * inv[i % half][:, None]).astype(np.float32).astype(np.float64)
    sign = np.where(i % 64 < half, -1.0, 1.0)[:, None]
    tables = np.stack([np.cos(ang), sign * np.sin(ang)], 1).astype(np.float32)
    return const, tables, dec


def weight_units(np, w_in, w_o, w_gate, w_up, w_down):
    L = w_in.shape[0]

    def tiles(w):
        n = w.shape[2] // P
        return w.reshape(L, KC, P, n, P).transpose(0, 3, 2, 1, 4).reshape(L, n, P, UNIT)

    gq, gk, gv, ga, gg, sq, sk, sv = np.split(w_in, [256, 512, 1024, 1040, 1552, 2064, 2192], axis=2)
    ga = np.concatenate([ga, ga, np.zeros((L, D_MODEL, P - 2 * RANK), w_in.dtype)], axis=2)
    sq = sq.reshape(L, D_MODEL, 2, 4, 64).transpose(0, 1, 3, 2, 4).reshape(L, D_MODEL, 512)
    wo_swa = w_o[:, 512:].reshape(L, 2, 4, 64, D_MODEL).transpose(0, 2, 1, 3, 4).reshape(L, 512, D_MODEL)
    wo = np.concatenate([w_o[:, :512], wo_swa], axis=1)
    gate, up = (tiles(w).reshape(L, FPAIRS, 2, 1, P, UNIT) for w in (w_gate, w_up))
    gu = np.concatenate([gate, up], axis=3).reshape(L, FPAIRS, 4, P, UNIT)
    down = w_down.reshape(L, FPAIRS, 2, P, 2, 4, P).transpose(0, 1, 4, 3, 2, 5, 6).reshape(L, FPAIRS, 2, P, UNIT)
    ff = np.concatenate([gu, down], axis=2).reshape(L, FPAIRS * 6, P, UNIT)
    return np.concatenate([tiles(w) for w in (sk, sv, sq, gk, gq, ga, gv, gg, wo)] + [ff], axis=1)


def layer_params(np, norm_attn, norm_ffn, gla_norm, b_gk2, attn_sinks):
    L = norm_attn.shape[0]
    cols = lambda a: a.reshape(L, -1, P).transpose(0, 2, 1)
    every = lambda a: np.broadcast_to(a[:, None, :], (L, P, a.shape[1]))
    rows = lambda a: np.repeat(a.reshape(L, 2, 4), NS, axis=2).transpose(0, 2, 1)
    return np.concatenate([cols(norm_attn), cols(norm_ffn), cols(gla_norm), cols(b_gk2),
                           every(attn_sinks), rows(attn_sinks)], axis=2)


def kernel(**inputs):
    import numpy as np
    import concourse.bacc as _bacc
    from concourse.bass_utils import run_bass_kernel_spmd as _run

    a = {k: np.asarray(v) for k, v in inputs.items()}
    L = DEPTH
    const, tables, dec = shape_constants(np)
    x_all = np.concatenate([a["x_prompt"].reshape(SEQ, D_MODEL), a["x_sample"].reshape(NS, D_MODEL)])
    arrays = {
        "x_t": x_all.reshape(T, KC, P).transpose(2, 1, 0),
        "units": weight_units(np, a["w_in"], a["w_o"], a["w_gate"], a["w_up"], a["w_down"]),
        "consts": const, "tables": tables, "dec_mask": dec,
        "params": layer_params(np, a["norm_attn"], a["norm_ffn"], a["gla_norm"], a["b_gk2"],
                               a["attn_sinks"]),
        "w_gk2": a["w_gk2"],
        "state_in": a["state_gla"].reshape(L, NB, GH * 64, P),
        "kcache_t": a["cache_swa_k"].reshape(L, NB, WCACHE, P).transpose(0, 3, 1, 2),
        "kcache": a["cache_swa_k"].reshape(L, NB, WCACHE, P),
        "vcache": a["cache_swa_v"].reshape(L, NB, WCACHE, P),
        "norm_final": a["norm_final"].reshape(KC, P).T,
    }
    arrays = {k: np.ascontiguousarray(v) for k, v in arrays.items()}
    outs = {
        "y_t": (P, KC, T), "state_p": (L, 1, GH * 64, P), "kc_p": (L, 1, WCACHE, P),
        "vc_p": (L, 1, WCACHE, P), "state_s": (L, NB, GH * 64, P), "kc_s": (L, NB, WCACHE, P),
        "vc_s": (L, NB, WCACHE, P),
    }
    nc = _bacc.Bacc("TRN2", target_bir_lowering=False, num_devices=1, dynamic_dma_scratch_size=256)
    args = [nc.dram_tensor(k, v.shape, mybir.dt.from_np(v.dtype), kind="ExternalInput").ap()
            for k, v in arrays.items()]
    args += [nc.dram_tensor("park", (P, KC - GH, T), mybir.dt.float32, kind="Internal").ap()]
    args += [nc.dram_tensor(k, s, mybir.dt.float32, kind="ExternalOutput").ap() for k, s in outs.items()]
    trunk(nc, *args)
    r = _run(nc, [arrays], core_ids=[0]).results[0]
    y = np.asarray(r["y_t"]).transpose(2, 1, 0).reshape(T, D_MODEL)
    cache = lambda name, n: np.asarray(r[name]).reshape(L, n, WCACHE, 2, 64)
    return (y[:SEQ].reshape(1, SEQ, D_MODEL), y[SEQ:].reshape(NB, NT, D_MODEL),
            np.asarray(r["state_p"]).reshape(L, 1, GH, 64, P), cache("kc_p", 1), cache("vc_p", 1),
            np.asarray(r["state_s"]).reshape(L, NB, GH, 64, P), cache("kc_s", NB), cache("vc_s", NB))
```
